# Optimizing a Trainium2 kernel written in Bass

```python
import math
import jax, jax.numpy as jnp
from jax import lax
import numpy as np

D_MODEL = 1024
BATCH = 1
SEQ = 1024
DEPTH = 1

HEAD_DIM = 64
SSM_WIDTH = 3 * D_MODEL // 8
FFT_WIDTH = D_MODEL // 4
ATT_WIDTH = D_MODEL - SSM_WIDTH - FFT_WIDTH
SSM_GROUP = 16
SSM_GROUPS = SSM_WIDTH // SSM_GROUP
SSM_STATE = 64
FFT_HEADS = FFT_WIDTH // HEAD_DIM
N_Q_HEADS = ATT_WIDTH // HEAD_DIM
N_KV_HEADS = 2
GQA_GROUP = N_Q_HEADS // N_KV_HEADS
KV_WIDTH = N_KV_HEADS * HEAD_DIM
IN_WIDTH = SSM_WIDTH + FFT_WIDTH + ATT_WIDTH + 2 * KV_WIDTH
WINDOW = 128
BLOCK = 128
KV_SPAN = 3 * BLOCK
D_FF = ((8 * D_MODEL // 3 + 255) // 256) * 256
DT_MIN = 1e-3
DT_MAX = 1e-1
RMS_EPS = 1e-6
NEG_INF = -1e30


def rms_norm(x, gain):
    xf = x.astype(jnp.float32)
    y = xf * lax.rsqrt(jnp.mean(xf * xf, axis=-1, keepdims=True) + RMS_EPS)
    return (y * gain.astype(jnp.float32)).astype(x.dtype)

def _scan_combine(left, right):
    a_l, h_l = left
    a_r, h_r = right
    return a_l * a_r, a_r * h_l + h_r

def s5_mixer(u, lam_re, lam_im, log_dt, b_re, b_im, c_re, c_im, d_skip, w_glu):
    bsz, seq, _ = u.shape
    f32 = jnp.float32
    uf = u.astype(f32).reshape(bsz, seq, SSM_GROUPS, SSM_GROUP)
    lam = lax.complex(lam_re.astype(f32), lam_im.astype(f32))
    dt = jnp.exp(log_dt.astype(f32))[..., None]
    lam_bar = jnp.exp(lam * dt)
    b = lax.complex(b_re.astype(f32), b_im.astype(f32))
    b_bar = ((lam_bar - 1.0) / lam)[..., None] * b
    states = []
    for d, rev in ((0, False), (1, True)):
        bu = lax.complex(jnp.einsum('bsgc,gpc->bsgp', uf, b_bar[d].real),
                         jnp.einsum('bsgc,gpc->bsgp', uf, b_bar[d].imag))
        a = jnp.broadcast_to(lam_bar[d], bu.shape)
        _, h_dir = lax.associative_scan(_scan_combine, (a, bu), reverse=rev, axis=1)
        states.append(h_dir)
    h = states[0] + states[1]
    y = (jnp.einsum('bsgp,gcp->bsgc', h.real, c_re.astype(f32))
         - jnp.einsum('bsgp,gcp->bsgc', h.imag, c_im.astype(f32)))
    y = y.reshape(bsz, seq, SSM_WIDTH) + d_skip.astype(f32) * u.astype(f32)
    y = jax.nn.gelu(y).astype(u.dtype)
    return y * jax.nn.sigmoid(y @ w_glu)

def fourier_mixer(f, w_fft):
    bsz, seq, _ = f.shape
    ff = f.astype(jnp.float32).reshape(bsz, seq, FFT_HEADS, HEAD_DIM)
    mixed = jnp.fft.fft2(ff, axes=(1, 3), norm='ortho').real.astype(f.dtype)
    return jnp.einsum('bshd,hde->bshe', mixed, w_fft).reshape(bsz, seq, FFT_WIDTH)

def window_attention(q, k, v, sink):
    bsz, seq, _ = q.shape
    nblk = seq // BLOCK
    qb = (q * HEAD_DIM ** -0.5).reshape(bsz, nblk, BLOCK, N_KV_HEADS, GQA_GROUP, HEAD_DIM)

    def band(t):
        t = t.reshape(bsz, seq, N_KV_HEADS, HEAD_DIM)
        t = jnp.pad(t, ((0, 0), (BLOCK, BLOCK), (0, 0), (0, 0)))
        t = t.reshape(bsz, nblk + 2, BLOCK, N_KV_HEADS, HEAD_DIM)
        return jnp.concatenate([t[:, :-2], t[:, 1:-1], t[:, 2:]], axis=2)

    kb, vb = band(k), band(v)
    qi = jnp.arange(BLOCK)[:, None]
    kj = jnp.arange(KV_SPAN)[None, :]
    dist = jnp.abs(qi + BLOCK - kj)
    key_pos = jnp.arange(nblk)[:, None] * BLOCK - BLOCK + kj
    valid = (dist <= WINDOW)[None] & ((key_pos >= 0) & (key_pos < seq))[:, None, :]
    slopes = jnp.exp2(-8.0 * jnp.arange(1, N_Q_HEADS + 1, dtype=jnp.float32) / N_Q_HEADS)
    slopes = slopes.reshape(N_KV_HEADS, GQA_GROUP)
    bias = -slopes[:, :, None, None] * dist.astype(jnp.float32)
    scores = jnp.einsum('bnqkgd,bnskd->bnkgqs', qb, kb).astype(jnp.float32) + bias
    scores = jnp.where(valid[None, :, None, None], scores, NEG_INF)
    sink_l = sink.astype(jnp.float32).reshape(1, 1, N_KV_HEADS, GQA_GROUP, 1, 1)
    m = jnp.maximum(jnp.max(scores, axis=-1, keepdims=True), sink_l)
    p = jnp.exp(scores - m)
    p = p / (jnp.sum(p, axis=-1, keepdims=True) + jnp.exp(sink_l - m))
    out = jnp.einsum('bnkgqs,bnskd->bnqkgd', p.astype(v.dtype), vb)
    return out.reshape(bsz, seq, ATT_WIDTH)

def dwconv3(h, w, b):
    hp = jnp.pad(h, ((0, 0), (1, 1), (0, 0)))
    return hp[:, :-2] * w[0] + hp[:, 1:-1] * w[1] + hp[:, 2:] * w[2] + b

def first_inputs(seed: int = 0) -> dict:
    key = jax.random.key(seed)
    ks = iter(jax.random.split(key, 32))
    nrm = lambda shape, scale: scale * jax.random.normal(next(ks), shape, jnp.float32)
    L, D, G, P = DEPTH, D_MODEL, SSM_GROUPS, SSM_STATE
    lam_im_base = jnp.pi * jnp.arange(P, dtype=jnp.float32)
    return {
        'x': nrm((BATCH, SEQ, D), 1.0),
        'c': nrm((BATCH, D), 1.0),
        'w_ada': nrm((L, D, 6 * D), 0.5 * D ** -0.5),
        'b_ada': nrm((L, 6 * D), 0.01),
        'g_pre_mix': 1.0 + nrm((L, D), 0.05),
        'g_post_mix': 1.0 + nrm((L, D), 0.05),
        'g_pre_ffn': 1.0 + nrm((L, D), 0.05),
        'g_post_ffn': 1.0 + nrm((L, D), 0.05),
        'w_in': nrm((L, D, IN_WIDTH), D ** -0.5),
        'lam_re': -0.5 + nrm((L, 2, G, P), 0.01),
        'lam_im': lam_im_base + nrm((L, 2, G, P), 0.01),
        'log_dt': jax.random.uniform(next(ks), (L, 2, G), jnp.float32,
                                     minval=math.log(DT_MIN), maxval=math.log(DT_MAX)),
        'b_re': nrm((L, 2, G, P, SSM_GROUP), (2 * SSM_GROUP) ** -0.5),
        'b_im': nrm((L, 2, G, P, SSM_GROUP), (2 * SSM_GROUP) ** -0.5),
        'c_re': nrm((L, G, SSM_GROUP, P), (2 * P) ** -0.5),
        'c_im': nrm((L, G, SSM_GROUP, P), (2 * P) ** -0.5),
        'd_skip': nrm((L, SSM_WIDTH), 1.0),
        'w_glu': nrm((L, SSM_WIDTH, SSM_WIDTH), SSM_WIDTH ** -0.5),
        'w_fft': nrm((L, FFT_HEADS, HEAD_DIM, HEAD_DIM), HEAD_DIM ** -0.5),
        'sink': nrm((L, N_Q_HEADS), 1.0),
        'w_out': nrm((L, D, D), D ** -0.5),
        'w_up': nrm((L, D, 2 * D_FF), D ** -0.5),
        'conv_w': nrm((L, 3, 2 * D_FF), 3 ** -0.5),
        'conv_b': nrm((L, 2 * D_FF), 0.01),
        'w_down': nrm((L, D_FF, D), D_FF ** -0.5),
    }

def first_block(x, c, w_ada, b_ada, g_pre_mix, g_post_mix, g_pre_ffn, g_post_ffn, w_in,
              lam_re, lam_im, log_dt, b_re, b_im, c_re, c_im, d_skip, w_glu, w_fft, sink,
              w_out, w_up, conv_w, conv_b, w_down):
    splits = [SSM_WIDTH, SSM_WIDTH + FFT_WIDTH, SSM_WIDTH + FFT_WIDTH + ATT_WIDTH,
              SSM_WIDTH + FFT_WIDTH + ATT_WIDTH + KV_WIDTH]
    for l in range(DEPTH):
        mod = (c @ w_ada[l] + b_ada[l])[:, None, :]
        sh_m, sc_m, gt_m, sh_f, sc_f, gt_f = jnp.split(mod, 6, axis=-1)

        h = rms_norm(x, g_pre_mix[l]) * (1.0 + sc_m) + sh_m
        z = h @ w_in[l]
        u, f, q, k, v = jnp.split(z, splits, axis=-1)
        y_ssm = s5_mixer(u, lam_re[l], lam_im[l], log_dt[l], b_re[l], b_im[l],
                         c_re[l], c_im[l], d_skip[l], w_glu[l])
        y_fft = fourier_mixer(f, w_fft[l])
        y_att = window_attention(q, k, v, sink[l])
        y = jnp.concatenate([y_ssm.astype(x.dtype), y_fft.astype(x.dtype), y_att.astype(x.dtype)], axis=-1) @ w_out[l]
        x = x + gt_m * rms_norm(y, g_post_mix[l])

        h = rms_norm(x, g_pre_ffn[l]) * (1.0 + sc_f) + sh_f
        up = dwconv3(h @ w_up[l], conv_w[l], conv_b[l])
        gate, val = jnp.split(up, 2, axis=-1)
        y = (jax.nn.gelu(gate) * val) @ w_down[l]
        x = x + gt_f * rms_norm(y, g_post_ffn[l])
    return x


PLE_DIM = 256
A_Q_HEADS = 8
A_KV_HEADS = 2
A_GROUP = A_Q_HEADS // A_KV_HEADS
A_WINDOW = 128
B_HEADS = 8
B_PATTERNS = ((128, 1), (512, 4), (2048, 16))
N_HEADS_TOTAL = A_Q_HEADS + B_HEADS
A_Q = A_Q_HEADS * HEAD_DIM
A_KV = A_KV_HEADS * HEAD_DIM
B_W = B_HEADS * HEAD_DIM
D_IN = A_Q + 2 * A_KV + 3 * B_W
D_MIX = A_Q + B_W
D_FF_2 = 2816
NUM_BUCKETS = 32
MAX_DISTANCE = 2048
EPS = 1e-6
NEG_INF_2 = -1e30


def rms_norm_2(x, g):
    xf = x.astype(jnp.float32)
    y = xf * lax.rsqrt(jnp.mean(xf * xf, axis=-1, keepdims=True) + EPS)
    return (y * g.astype(jnp.float32)).astype(x.dtype)

def swiglu(x, w_gu, w_down):
    g, u = jnp.split(x @ w_gu, 2, axis=-1)
    return (jax.nn.silu(g) * u) @ w_down

def t5_bucket(dist):
    max_exact = NUM_BUCKETS // 2
    n = jnp.maximum(dist, 0)
    nf = jnp.maximum(n, 1).astype(jnp.float32)
    large = max_exact + (jnp.log(nf / max_exact) / math.log(MAX_DISTANCE / max_exact)
                         * (NUM_BUCKETS - max_exact)).astype(jnp.int32)
    large = jnp.minimum(large, NUM_BUCKETS - 1)
    return jnp.where(n < max_exact, n, large)

def banded_attention(q, k, v, rel_bias, max_dist, stride):
    n, L, hkv, grp, dh = q.shape
    bq = math.gcd(L, BLOCK)
    nb = L // bq
    nk = bq + max_dist
    pad = ((0, 0), (max_dist, 0), (0, 0), (0, 0))
    k_pad = jnp.pad(k, pad)
    v_pad = jnp.pad(v, pad)
    key_idx = jnp.arange(nb)[:, None] * bq + jnp.arange(nk)[None, :]
    kb = k_pad[:, key_idx]
    vb = v_pad[:, key_idx]
    qb = q.reshape(n, nb, bq, hkv, grp, dh)
    logits = jnp.einsum('nbqhgd,nbkhd->nbhgqk', qb, kb,
                        preferred_element_type=jnp.float32) * (dh ** -0.5)
    rel = jnp.arange(bq)[:, None] + max_dist - jnp.arange(nk)[None, :]
    bias = rel_bias[t5_bucket(rel * stride)].astype(jnp.float32)
    bias = bias.reshape(bq, nk, hkv, grp).transpose(2, 3, 0, 1)
    in_band = (rel >= 0) & (rel <= max_dist)
    key_pos = key_idx - max_dist
    valid = in_band[None] & (key_pos >= 0)[:, None, :]
    logits = jnp.where(valid[None, :, None, None], logits + bias, NEG_INF_2)
    m = jnp.max(logits, axis=-1)
    pr = jnp.exp(logits - m[..., None])
    s = jnp.sum(pr, axis=-1)
    o = jnp.einsum('nbhgqk,nbkhd->nbqhgd', pr, vb.astype(jnp.float32))
    o = o.reshape(n, L, hkv, grp, dh)
    m = m.transpose(0, 1, 4, 2, 3).reshape(n, L, hkv, grp)
    s = s.transpose(0, 1, 4, 2, 3).reshape(n, L, hkv, grp)
    return o, m, s

def to_classes(t, r):
    b, s = t.shape[:2]
    rest = t.shape[2:]
    t = jnp.moveaxis(t.reshape((b, s // r, r) + rest), 2, 1)
    return t.reshape((b * r, s // r) + rest)

def from_classes(t, b, r):
    n, L = t.shape[:2]
    rest = t.shape[2:]
    t = jnp.moveaxis(t.reshape((b, r, L) + rest), 1, 2)
    return t.reshape((b, L * r) + rest)

def sink_swa_gqa(q_a, k_a, v_a, sinks, rel_bias_a):
    b, s, _ = q_a.shape
    q = q_a.reshape(b, s, A_KV_HEADS, A_GROUP, HEAD_DIM)
    k = k_a.reshape(b, s, A_KV_HEADS, HEAD_DIM)
    v = v_a.reshape(b, s, A_KV_HEADS, HEAD_DIM)
    o, m, den = banded_attention(q, k, v, rel_bias_a, A_WINDOW - 1, 1)
    sink = sinks.reshape(A_KV_HEADS, A_GROUP).astype(jnp.float32)
    m_all = jnp.maximum(m, sink)
    scale = jnp.exp(m - m_all)
    total = den * scale + jnp.exp(sink - m_all)
    o = o * (scale / total)[..., None]
    return o.reshape(b, s, A_Q)

def dilated_mixture(q_b, k_b, v_b, rel_bias_b):
    b, s, _ = q_b.shape
    q = q_b.reshape(b, s, B_HEADS, 1, HEAD_DIM)
    k = k_b.reshape(b, s, B_HEADS, HEAD_DIM)
    v = v_b.reshape(b, s, B_HEADS, HEAD_DIM)
    outs, maxes, dens = [], [], []
    for window, dil in B_PATTERNS:
        o, m, den = banded_attention(to_classes(q, dil), to_classes(k, dil), to_classes(v, dil),
                                     rel_bias_b, window // dil, dil)
        outs.append(from_classes(o, b, dil))
        maxes.append(from_classes(m, b, dil))
        dens.append(from_classes(den, b, dil))
    m_stack = jnp.stack(maxes)
    m_all = jnp.max(m_stack, axis=0)
    w = jnp.exp(m_stack - m_all)
    num = jnp.sum(w[..., None] * jnp.stack(outs), axis=0)
    den_all = jnp.sum(w * jnp.stack(dens), axis=0)
    return (num / den_all[..., None]).reshape(b, s, B_W)

def second_inputs(seed: int = 0) -> dict:
    key = jax.random.key(seed)
    ks = jax.random.split(key, 24)
    f32 = jnp.float32

    def w(k, shape, fan_in):
        return jax.random.normal(k, shape, f32) * (fan_in ** -0.5)

    def gain(k, shape):
        return 1.0 + 0.05 * jax.random.normal(k, shape, f32)

    def small(k, shape, scale=0.02):
        return scale * jax.random.normal(k, shape, f32)

    D = D_MODEL
    return {
        "x": jax.random.normal(ks[0], (BATCH, SEQ, D), f32),
        "p": jax.random.normal(ks[1], (DEPTH, BATCH, SEQ, PLE_DIM), f32),
        "rel_bias": small(ks[2], (NUM_BUCKETS, N_HEADS_TOTAL), 0.5),
        "ffn1_pre_g": gain(ks[3], (DEPTH, D)),
        "ffn1_w_gu": w(ks[4], (DEPTH, D, 2 * D_FF_2), D),
        "ffn1_w_down": w(ks[5], (DEPTH, D_FF_2, D), D_FF_2),
        "ffn1_post_g": gain(ks[6], (DEPTH, D)),
        "attn_pre_g": gain(ks[7], (DEPTH, D)),
        "w_in": w(ks[8], (DEPTH, D, D_IN), D),
        "b_in": small(ks[9], (DEPTH, D_IN)),
        "sinks": small(ks[10], (DEPTH, A_Q_HEADS), 0.5),
        "w_out": w(ks[11], (DEPTH, D_MIX, D), D_MIX),
        "b_out": small(ks[12], (DEPTH, D)),
        "attn_post_g": gain(ks[13], (DEPTH, D)),
        "ffn2_pre_g": gain(ks[14], (DEPTH, D)),
        "ffn2_w_gu": w(ks[15], (DEPTH, D, 2 * D_FF_2), D),
        "ffn2_w_down": w(ks[16], (DEPTH, D_FF_2, D), D_FF_2),
        "ffn2_post_g": gain(ks[17], (DEPTH, D)),
        "ple_pre_g": gain(ks[18], (DEPTH, D)),
        "w_ple_gate": w(ks[19], (DEPTH, D, D), D),
        "w_ple_proj": w(ks[20], (DEPTH, PLE_DIM, D), PLE_DIM),
        "ple_post_g": gain(ks[21], (DEPTH, D)),
    }

def second_block(x, p, rel_bias, ffn1_pre_g, ffn1_w_gu, ffn1_w_down, ffn1_post_g,
              attn_pre_g, w_in, b_in, sinks, w_out, b_out, attn_post_g,
              ffn2_pre_g, ffn2_w_gu, ffn2_w_down, ffn2_post_g,
              ple_pre_g, w_ple_gate, w_ple_proj, ple_post_g):
    h = x
    splits = [A_Q, A_Q + A_KV, A_Q + 2 * A_KV, A_Q + 2 * A_KV + B_W, A_Q + 2 * A_KV + 2 * B_W]
    for i in range(DEPTH):
        f = swiglu(rms_norm_2(h, ffn1_pre_g[i]), ffn1_w_gu[i], ffn1_w_down[i])
        h = h + 0.5 * rms_norm_2(f, ffn1_post_g[i])

        z = rms_norm_2(h, attn_pre_g[i]) @ w_in[i] + b_in[i]
        q_a, k_a, v_a, q_b, k_b, v_b = jnp.split(z, splits, axis=-1)
        out_a = sink_swa_gqa(q_a, k_a, v_a, sinks[i], rel_bias[:, :A_Q_HEADS])
        out_b = dilated_mixture(q_b, k_b, v_b, rel_bias[:, A_Q_HEADS:])
        mix = jnp.concatenate([out_a, out_b], axis=-1).astype(x.dtype)
        att = mix @ w_out[i] + b_out[i]
        h = h + rms_norm_2(att, attn_post_g[i])

        f = swiglu(rms_norm_2(h, ffn2_pre_g[i]), ffn2_w_gu[i], ffn2_w_down[i])
        h = h + 0.5 * rms_norm_2(f, ffn2_post_g[i])

        gate = jax.nn.sigmoid(rms_norm_2(h, ple_pre_g[i]) @ w_ple_gate[i])
        e = p[i] @ w_ple_proj[i]
        h = h + rms_norm_2(gate * e, ple_post_g[i])
    return h


def setup_inputs(seed=0):
    out = dict(first_inputs(seed))
    for name, value in second_inputs(seed + 1).items():
        if name != "x":
            out[name + "_2"] = value
    return out


def reference(
    x, c, w_ada, b_ada, g_pre_mix, g_post_mix, g_pre_ffn, g_post_ffn, w_in, lam_re, lam_im,
    log_dt, b_re, b_im, c_re, c_im, d_skip, w_glu, w_fft, sink, w_out, w_up, conv_w, conv_b,
    w_down, p_2, rel_bias_2, ffn1_pre_g_2, ffn1_w_gu_2, ffn1_w_down_2, ffn1_post_g_2,
    attn_pre_g_2, w_in_2, b_in_2, sinks_2, w_out_2, b_out_2, attn_post_g_2, ffn2_pre_g_2,
    ffn2_w_gu_2, ffn2_w_down_2, ffn2_post_g_2, ple_pre_g_2, w_ple_gate_2, w_ple_proj_2,
    ple_post_g_2,
):
    x = first_block(
        x, c, w_ada, b_ada, g_pre_mix, g_post_mix, g_pre_ffn, g_post_ffn, w_in, lam_re, lam_im,
        log_dt, b_re, b_im, c_re, c_im, d_skip, w_glu, w_fft, sink, w_out, w_up, conv_w, conv_b,
        w_down,
    )
    return second_block(
        x, p_2, rel_bias_2, ffn1_pre_g_2, ffn1_w_gu_2, ffn1_w_down_2, ffn1_post_g_2,
        attn_pre_g_2, w_in_2, b_in_2, sinks_2, w_out_2, b_out_2, attn_post_g_2, ffn2_pre_g_2,
        ffn2_w_gu_2, ffn2_w_down_2, ffn2_post_g_2, ple_pre_g_2, w_ple_gate_2, w_ple_proj_2,
        ple_post_g_2,
    )


_drawn_inputs = setup_inputs


def setup_inputs(seed=0):
    import zlib

    import numpy as np

    out = dict(_drawn_inputs(seed))
    spreads = {}
    factors = {'b_ada': 2.981,
     'lam_re': 64.0,
     'log_dt': 24.352,
     'conv_b': 8.0,
     'ffn1_post_g_2': 3.534,
     'sinks_2': 8.0,
     'ffn2_pre_g_2': 3.091,
     'ffn2_post_g_2': 4.49,
     'ple_pre_g_2': 23.616,
     'lam_im': 8.0,
     'b_re': 8.0,
     'b_im': 8.0,
     'c_re': 8.0,
     'c_im': 8.0,
     'ple_post_g_2': 3.883}
    for name, (base, spread) in spreads.items():
        noise = np.random.default_rng([zlib.crc32(name.encode()), seed]).standard_normal(out[name].shape)
        drawn = base * np.exp(spread * noise) if base else spread * noise
        out[name] = __import__('jax').numpy.asarray(drawn.astype(out[name].dtype))
    for name, factor in factors.items():
        out[name] = (out[name] * factor).astype(out[name].dtype)
    return out
```

```python
from contextlib import ExitStack

import concourse.bass as bass
from concourse import mybir

F32, F32R = mybir.dt.float32, mybir.dt.float32r
ACT, ALU, AX = mybir.ActivationFunctionType, mybir.AluOpType, mybir.AxisListType
P = 128
KB = 1024
SBUF0 = 16512
SEQ, D, HD = 1024, 1024, 64
KT = D // P
TT = SEQ // P
FF = 2816
FT = FF // P
SSM_W, G, GC, NST, GSUB = 384, 24, 16, 64, 4
CH = 8
NCH = SEQ // CH
EPS = 1e-6
NEG = -1e30
NBUF = 3
BUCKETS = 32
W_B, W_A = 1152, 384
ds = bass.ds


def repeat(e, n, u, body):
    turns = n // u
    if turns > 1:
        with e.Fori(0, turns) as i:
            for j in range(u):
                body(i * u + j, j, i)
    else:
        for j in range(turns * u):
            body(j, j, 0)
    for j in range(turns * u, n):
        body(j, j % u, j // u)


def wait(e, sem, value):
    if not isinstance(value, int) or value > 0:
        e.wait_ge(sem, value)


def wait_alone(e, sem, value, passed):
    if not isinstance(value, int):
        value = e.to_reg(value)
        e.wait_ge(passed, 1)
    wait(e, sem, value)


class Chain:

    def __init__(self, e, sem, base=0, passed=None):
        self.e, self.sem, self.base, self.passed, self.n = e, sem, base, passed, 0

    def then(self, ins):
        ins.then_inc(self.sem, 1)
        self.n += 1
        if self.passed:
            wait_alone(self.e, self.sem, self.base + self.n, self.passed)
        else:
            self.e.wait_ge(self.sem, self.base + self.n)


def vector_rows(t):
    r = lambda ap: ap.rearrange("a (r c) -> (a r) c", c=P)
    return [("conv_w", t["conv_w"].rearrange("l t (r c) -> (l t r) c", c=P)), ("conv_b", r(t["conv_b"])),
            ("c", r(t["c"])), ("b_ada", r(t["b_ada"])),
            ("g_pre_mix", r(t["g_pre_mix"])), ("g_pre_ffn", r(t["g_pre_ffn"])),
            ("g_post_mix", r(t["g_post_mix"])), ("g_post_ffn", r(t["g_post_ffn"])),
            ("ffn1_pre", r(t["ffn1_pre_g_2"])), ("attn_pre", r(t["attn_pre_g_2"])),
            ("ffn2_pre", r(t["ffn2_pre_g_2"])), ("ple_pre", r(t["ple_pre_g_2"])), ("b_in", r(t["b_in_2"]))]


def build(nc, t, out, last=6):
    ctx = ExitStack()
    with ctx:
        def at(name, shape, dt, off):
            return nc.alloc_sbuf_tensor_at(name, shape, dt, offset=SBUF0 + int(off))

        sems = {}

        def S(name):
            if name not in sems:
                sems[name] = ctx.enter_context(nc.semaphore(name))
            return sems[name]

        def dram(name, shape):
            return nc.dram_tensor(name, shape, F32, kind="Internal").ap()

        R1, R2, R3 = 88 * KB, 152 * KB, 200 * KB
        xs = dram("xs", (SEQ, D))
        grow = dram("grow", (2, D))
        qk = dram("qk", (9 * P + 4 * P, SEQ))
        vs = dram("vs", (SEQ, 640))
        kpd = dram("kpd", (GSUB, GC, 15 * GC))
        tabd = dram("tabd", (16, P, W_B))

        w_raw = [at(f"w_raw{b}", [P, 2048], F32, R2 + b * 16 * KB) for b in range(NBUF)]
        w_lo = [at(f"w_lo{b}", [P, 2048], F32R, R2 + b * 16 * KB) for b in range(NBUF)]
        w_hi = [at(f"w_hi{b}", [P, 2048], F32R, R2 + b * 16 * KB + 8 * KB) for b in range(NBUF)]
        act1 = at("act1", [P, SEQ], F32, R3)
        ident = at("ident", [P, P], F32, R3 + 4096)
        vec = at("vec", [P, 384], F32, R3 + 4608)
        mod = at("mod", [P, 48], F32, R3 + 6144)
        gain1 = at("gain1", [P, 32], F32, R3 + 6336)
        stat = at("stat", [P, 6, 8], F32, R3 + 6464)
        junk = at("junk", [P, 2], F32, R3 + 6656)
        epsc = at("epsc", [P, 2], F32, R3 + 6688)
        h_hi = at("h_hi", [P, KT, SEQ], F32R, R1)
        h_lo = at("h_lo", [P, KT, SEQ], F32R, R1 + 32 * KB)
        y_hi = at("y_hi", [P, KT, SEQ], F32R, R1)
        y_lo = at("y_lo", [P, KT, SEQ], F32R, R1 + 32 * KB)
        xn = at("xn", [P, TT, D], F32, 0)
        aT = at("aT", [P, FT, SEQ], F32, 0)
        fold = [at(f"fold{i}", [P, 512], F32, 84 * KB + i * 2 * KB) for i in range(2)]
        a_hi = [at(f"a_hi{b}", [P, 2, 512], F32R, R1 + b * 8 * KB) for b in range(3)]
        a_lo = [at(f"a_lo{b}", [P, 2, 512], F32R, R1 + b * 8 * KB + 4 * KB) for b in range(3)]
        class Post:
            def __init__(self, n, off):
                self.x = at(f"px{n}", [P, TT, D], F32, off)
                self.g = at(f"pg{n}", [P, D], F32, off + 32 * KB)
                self.tmp = at(f"pt{n}", [P, D], F32, off + 36 * KB)
                if n == 0:
                    self.bias = at("pb0", [P, D], F32, off + 40 * KB)
                    self.y = at("py0", [P, D], F32, off + 44 * KB)
        post_m, post_f = Post(0, 32 * KB), Post(1, R1 + 24 * KB)

        PS = ctx.enter_context(nc.psum_tensor("PS", [P, 8, 512], F32))
        PSr = PS[:].rearrange("p b n -> p (b n)")

        segs = []

        def seg(name, kind, ap, n):
            g0 = sum(s[3] for s in segs)
            segs.append((name, kind, ap, n, g0))
            return g0

        cols = lambda w: w[0].rearrange("(k p) n -> p k n", p=P)
        rows = lambda w: w.rearrange("(m k p) n -> m p k n", p=P, k=2)
        G_Z1 = seg("z1", "cols", cols(t["w_in"]), 5)
        G_DFT = seg("dft", "rows", rows(t["dft"]), 8)
        G_GLU = seg("glu", "glu", t["w_glu"][0].rearrange("(k p) n -> p k n", p=P), 1)
        G_OUT1 = [seg("out1", "rows", rows(t["w_out"][0]), 4) for _ in range(2)]
        G_UP = [seg("up0", "pair", cols(t["w_up"]), FT)]
        G_DN = [[seg("dn0", "rows", rows(t["w_down"][0]), FT // 2) for _ in range(2)]]
        G_UP += [seg("up1", "pair", cols(t["ffn1_w_gu_2"]), FT)]
        G_DN += [[seg("dn1", "rows", rows(t["ffn1_w_down_2"][0]), FT // 2) for _ in range(2)]]
        G_Z2 = seg("z2", "cols", cols(t["w_in_2"]), 9)
        G_OUT2 = [seg("out2", "rows", rows(t["w_out_2"][0]), 4) for _ in range(2)]
        G_UP += [seg("up2", "pair", cols(t["ffn2_w_gu_2"]), FT)]
        G_DN += [[seg("dn2", "rows", rows(t["ffn2_w_down_2"][0]), FT // 2) for _ in range(2)]]
        G_PLE = []
        for _ in range(2):
            g = seg("gate", "rows", rows(t["w_ple_gate_2"][0]), 4)
            seg("proj", "rows", rows(t["w_ple_proj_2"][0]), 1)
            G_PLE.append(g)
        g_end = {1: G_UP[0], 2: G_UP[1], 3: G_Z2, 4: G_UP[2], 5: G_PLE[0]}.get(last, sum(s[3] for s in segs))
        segs = [s for s in segs if s[4] < g_end]

        def w_view(b, kind, which):
            v = {"raw": w_raw, "hi": w_hi, "lo": w_lo}[which][b]
            if kind == "cols":
                return v[:].rearrange("p (k n) -> p k n", k=8)
            if kind == "rows":
                return v[:].rearrange("p (k n) -> p k n", k=2)
            return v[:, 0:3 * SSM_W].rearrange("p (k n) -> p k n", k=3)

        def load_chunk(e, kind, ap, i, g, b):
            wait_alone(e, S("w_used"), g + 1 - NBUF, S("idc"))
            dst = w_view(b, "cols" if kind == "pair" else kind, "raw")
            for h in range(2):
                if kind == "cols":
                    to, src = dst[:, 4 * h:4 * h + 4, :], ap[:, 4 * h:4 * h + 4, ds(i * 256, 256)]
                elif kind == "pair":
                    to, src = dst[:, :, h * P:h * P + P], ap[:, :, ds(i * P + h * FF, P)]
                elif kind == "rows":
                    to, src = dst[:, h, :], ap[ds(i, 1), :, h, :].rearrange("o p n -> p (o n)")
                else:
                    to, src = (dst[:, 0:2, :], ap[:, 0:2, :]) if h == 0 else (dst[:, 2, :], ap[:, 2, :])
                e.dma_start(to, src).then_inc(S(f"w_loaded{b}"), 16)

        def stream_load(e, first, end):
            for _, kind, ap, n, g0 in segs:
                lo, hi = max(first, g0), min(end, g0 + n)
                if lo < hi:
                    repeat(e, hi - lo, NBUF, lambda i, j, turn: load_chunk(
                        e, kind, ap, i + (lo - g0), i + lo, (lo + j) % NBUF))

        def stream_split(e, first, end):
            def body(i, j, turn, g0, n):
                b = (g0 + j) % NBUF
                wait_alone(e, S(f"w_loaded{b}"), turn * 32 + 32 * ((g0 + j) // NBUF + 1), S("idc"))
                e.tensor_copy(w_hi[b][:, 0:n], w_raw[b][:, 0:n]).then_inc(S("w_hi"), 1)
                wait_alone(e, S("w_hi"), i + (g0 + 1), S("idc"))
                e.tensor_tensor(w_lo[b][:, 0:n], w_raw[b][:, 0:n], w_hi[b][:, 0:n].bitcast(F32), ALU.subtract)\
                 .then_inc(S("w_split"), 1)
            end = min(end, g_end)
            if first <= G_GLU < end:
                stream_split(e, first, G_GLU)
                body(0, 0, 0, G_GLU, 3 * SSM_W)
                first = G_GLU + 1
            if first < end:
                repeat(e, end - first, NBUF, lambda i, j, turn: body(i, j, turn, first, 2048))

        rows_of = vector_rows(t)
        VC, r0 = {}, 0
        for name, ap in rows_of:
            VC[name] = r0
            r0 += ap.shape[0]
        NV = r0
        vrow = at("vrow", [P, 3, P], F32, R1)
        ada = [at(f"ada{b}", [P, 4, D], F32, 32 * KB + b * 16 * KB) for b in range(2)]
        oh_b = at("oh_b", [BUCKETS + 1, W_B], F32, R1 + 2 * KB)
        oh_a = at("oh_a", [BUCKETS + 1, W_A], F32, R1 + 7 * KB)
        relb = at("relb", [BUCKETS, 16], F32, R1 + 9 * KB)
        relbb = at("relbb", [BUCKETS + 1, 16, P], F32, R1 + 10 * KB)
        tst = [at(f"tst{i}", [P, W_B], F32, R1 + 18 * KB + i * 5 * KB) for i in range(2)]
        NQ = 23
        WR, WI, RHO, C8, S8, PR, PI, PRD, PID = 0, 1, 2, 3, 4, 5, 14, 23, 32
        pw = at("pw", [2 * G, NQ, P], F32, R1 + 28 * KB)
        sx = [at(f"sx{i}", [2 * G, P], F32, R1 + 40 * KB + i * 512) for i in range(20)]
        ldt = at("ldt", [2 * G, 2], F32, R1 + 51 * KB)
        crow = [at(f"crow{i}", [P, 3, P], F32, R1 + 52 * KB + i * 1536) for i in range(2)]
        braw = [at(f"braw{i}", [P, 2, G, GC], F32, R1 + 55 * KB + i * 3 * KB) for i in range(2)]
        stn = at("stn", [P, 41, 2 * G], F32, 64 * KB)
        bb = [at(f"bb{i}", [P, 2 * G, GC], F32, 72 * KB + i * 3 * KB) for i in range(2)]
        cc = [at(f"cc{i}", [P, SSM_W], F32, 78 * KB + i * 1536) for i in range(2)]
        sgn = at("sgn", [P, 2], F32, 81 * KB)
        btmp = [at(f"btmp{i}", [P, 2 * G, GC], F32, R1 + 40 * KB + i * 3 * KB) for i in range(2)]
        gcol = lambda i: gain1[:, i:i + 1]
        vcol = lambda name, i: vec[:, VC[name] + i:VC[name] + i + 1]

        def rows_dma(e):
            n = 0
            for name, ap in rows_of:
                r, done = VC[name], 0
                while done < ap.shape[0]:
                    k = min(ap.shape[0] - done, P - (r + done) % P)
                    e.dma_start(vrow[(r + done) % P:(r + done) % P + k, (r + done) // P, :],
                                ap[done:done + k, :]).then_inc(S("vr_ld"), 16)
                    done += k
                    n += 1
            return n

        def prep_sp(e):
            n = rows_dma(e)
            e.dma_start(oh_b[:], t["oh_b"]).then_inc(S("oh_ld"), 16)
            e.dma_start(oh_a[:], t["oh_a"]).then_inc(S("oh_ld"), 16)
            e.dma_start(relb[:], t["rel_bias_2"]).then_inc(S("oh_ld"), 16)
            stream_load(e, 0, NBUF)
            w = t["w_ada"][0].rearrange("(h k p) n -> h p k n", p=P, h=2)
            for c in range(12):
                if c >= 2:
                    e.wait_ge(S("ada_mm"), c - 1)
                e.dma_start(ada[c % 2][:], w[c % 2, :, :, (c // 2) * D:(c // 2 + 1) * D])\
                 .then_inc(S(f"ada_ld{c % 2}"), 16)
                if c == 1:
                    e.dma_start(xn[:], t["x"][0].rearrange("(t p) n -> p t n", p=P)).then_inc(S("x0_ld"), 16)
            return n

        N_VR = sum(-(-(VC[n] % P + ap.shape[0]) // P) for n, ap in rows_of)

        def prep_pool(e):
            ch = Chain(e, S("idc"))
            ch.then(e.memset(ident[:], 0.0))
            ch.then(e.memset(relbb[BUCKETS:BUCKETS + 1, :, :], 1.0))
            for r, v in ((slice(0, NST), 1.0), (slice(NST, P), -1.0)):
                ch.then(e.memset(sgn[r, 0:1], v))
                ch.then(e.memset(sgn[r, 1:2], -v))
            ch.then(e.affine_select(out=ident[:], in_=ident[:], compare_op=ALU.not_equal, fill=1.0, base=0,
                                    pattern=[[-1, P]], channel_multiplier=1))

        def prep_act(e):
            for h in range(2):
                e.dma_start(sx[0][:, h * NST:(h + 1) * NST], t["lam_re"][0].rearrange("d g p -> (d g) p"))\
                 .then_inc(S("sp_ld"), 16)
                e.dma_start(sx[1][:, h * NST:(h + 1) * NST], t["lam_im"][0].rearrange("d g p -> (d g) p"))\
                 .then_inc(S("sp_ld"), 16)
            e.dma_start(ldt[:, 0:1], t["log_dt"][0].rearrange("d (g o) -> (d g) o", o=1)).then_inc(S("sp_ld"), 16)
            cr, ci = (t[n][0].rearrange("g c p -> (g c) p").rearrange("(m r) p -> r m p", r=P) for n in ("c_re", "c_im"))
            for k, pair in enumerate(((cr, ci), (ci, cr))):
                for h in range(2):
                    e.dma_start(crow[k][:, :, h * NST:(h + 1) * NST], pair[h]).then_inc(S("sp_ld"), 16)
            for k, pair in enumerate((("b_re", "b_im"), ("b_im", "b_re"))):
                for h in range(2):
                    for d in range(2):
                        e.dma_start(braw[k][h * NST:(h + 1) * NST, d, :, :],
                                    t[pair[h]][0, d].rearrange("g p c -> p g c")).then_inc(S("sp_ld"), 16)
            e.wait_ge(S("sp_ld"), 16 * N_SP)
            e.activation(ldt[:, 1:2], ldt[:, 0:1], ACT.Exp).then_inc(S("sp_dt"), 1)
            for h in range(16):
                w = W_A if h < 8 else W_B
                e.wait_ge(S("tb_mm"), h + 1)
                if h >= 2:
                    e.wait_ge(S(f"tb_st{h % 2}"), 16 * (h // 2))
                e.activation(tst[h % 2][:, 0:w], PSr[:, 512:512 + w], ACT.Copy).then_inc(S("tb_ev"), 1)
                e.wait_ge(S("tb_ev"), h + 1)
                e.dma_start(tabd[h, :, 0:w], tst[h % 2][:, 0:w]).then_inc(S(f"tb_st{h % 2}"), 16)

        N_SP = 5 + 4 + 8

        def prep_pe(e):
            e.wait_ge(S("vr_ld"), 16 * N_VR)
            e.wait_ge(S("idc"), 7)
            for m in range(3):
                k = min(P, NV - m * P)
                mm = e.transpose(PS[:, 0, m * P:m * P + k], vrow[0:k, m, :], ident[0:k, 0:k])
            mm.then_inc(S("vc_t"), 1)

            def bias_rows(h):
                e.wait_ge(S("rb"), 1)
                wait(e, S("tb_ev"), h)
                w, oh = (W_A, oh_a) if h < 8 else (W_B, oh_b)
                for c in range(0, w, 512):
                    mm = e.matmul(PSr[:, 512 + c:512 + min(c + 512, w)], relbb[:, h, :], oh[:, c:min(c + 512, w)],
                                  start=True, stop=True)
                mm.then_inc(S("tb_mm"), 1)

            for c in range(12):
                e.wait_ge(S("vc"), 1)
                e.wait_ge(S(f"ada_ld{c % 2}"), 16 * (c // 2 + 1))
                for m in range(KT):
                    for k in range(4):
                        mm = e.matmul(PS[:, 7, (c // 2) * 8 + m:(c // 2) * 8 + m + 1], ada[c % 2][:, k, m * P:(m + 1) * P],
                                      vcol("c", (c % 2) * 4 + k), start=(c == 0 and m == 0 and k == 0),
                                      stop=(c == 11 and m == 7 and k == 3), skip_group_check=True)
                mm.then_inc(S("ada_mm"), 1)
                if c < 11:
                    bias_rows(c)
                if c == 3:
                    e.wait_ge(S("sp_ld"), 16 * N_SP)
                    for i in range(2):
                        for m in range(3):
                            mm = e.transpose(PS[:, 4 + i, m * P:(m + 1) * P], crow[i][:, m, :], ident[:])
                    mm.then_inc(S("c_t"), 1)
            for h in range(11, 16):
                bias_rows(h)
            e.wait_ge(S("pw"), 1)
            e.wait_ge(S("cc"), 2)
            for q in range(NQ):
                mm = e.transpose(PS[:, 4 + q // 10, (q % 10) * 48:(q % 10) * 48 + 48], pw[:, q, :], ident[0:48, 0:48])
            mm.then_inc(S("pw_t"), 1)
            e.wait_ge(S("gts"), 1)
            e.transpose(PS[0:16, 0, 0:P], gain1[:, 16:32], ident[:]).then_inc(S("gr_t"), 1)

        def prep_dve(e):
            for i in range(2):
                e.memset(junk[:, i:i + 1], 0.0).then_inc(S("f_out"), 1)
            e.wait_ge(S("f_out"), 2)
            e.memset(epsc[:, 0:1], EPS).then_inc(S("eps"), 1)
            e.memset(epsc[:, 1:2], 4 * EPS).then_inc(S("eps"), 1)
            e.wait_ge(S("vc_t"), 1)
            e.tensor_copy(vec[:, 0:NV], PS[:, 0, 0:NV]).then_inc(S("vc"), 1)
            e.wait_ge(S("oh_ld"), 48)
            e.wait_ge(S("idc"), 7)
            e.tensor_copy(relbb[0:BUCKETS, :, :], relb[:].unsqueeze(2).to_broadcast([BUCKETS, 16, P])).then_inc(S("rb"), 1)
            ch = Chain(e, S("spd"))
            lre, lim = sx[0][:], sx[1][:]
            X, TH, Q, Y, A, B, W2, T0, T1, M = (sx[i][:] for i in range(2, 12))
            e.wait_ge(S("sp_dt"), 1)
            ts = lambda o, i, s0, s1, *ops: ch.then(e.tensor_scalar(o, i, s0, s1, *ops))
            tt = lambda o, a, b, op: ch.then(e.tensor_tensor(o, a, b, op))
            stt = lambda o, a, s, b, o0, o1: ch.then(e.scalar_tensor_tensor(o, a, s, b, o0, o1))
            ts(X, lre, ldt[:, 1:2], None, ALU.mult)
            ts(TH, lim, ldt[:, 1:2], None, ALU.mult)
            ts(X, X, 88.0, -100.0, ALU.min, ALU.max)
            ts(Y, X, 1.0 / 128, None, ALU.mult)
            ts(M, Y, 1.0 / 9, None, ALU.mult)
            for k in range(8, 0, -1):
                stt(M, M, 1.0, Y, ALU.add, ALU.mult)
                if k > 1:
                    ts(M, M, 1.0 / k, None, ALU.mult)
            for _ in range(7):
                stt(M, M, 2.0, M, ALU.add, ALU.mult)
            ts(Q, TH, 0.15915494309189535, 12582912.0, ALU.mult, ALU.add)
            ts(Q, Q, 12582912.0, None, ALU.subtract)
            for c in (6.28125, 0.0019350051879882812, 3.0199159819800e-07):
                stt(TH, Q, -c, TH, ALU.mult, ALU.add)
            ts(Y, TH, 0.125, None, ALU.mult)
            tt(W2, Y, Y, ALU.mult)
            ts(B, W2, -1.0 / 72, 1.0, ALU.mult, ALU.add)
            for c in (42, 20, 6):
                tt(B, B, W2, ALU.mult)
                ts(B, B, -1.0 / c, 1.0, ALU.mult, ALU.add)
            tt(B, B, Y, ALU.mult)
            ts(A, W2, -1.0 / 56, 1.0, ALU.mult, ALU.add)
            for c in (30, 12):
                tt(A, A, W2, ALU.mult)
                ts(A, A, -1.0 / c, 1.0, ALU.mult, ALU.add)
            stt(A, A, -0.5, W2, ALU.mult, ALU.mult)

            def double():
                stt(T0, A, 1.0, B, ALU.add, ALU.mult)
                stt(A, B, -2.0, B, ALU.mult, ALU.mult)
                ts(B, T0, 2.0, None, ALU.mult)

            for _ in range(3):
                double()
            LR, LI = T1, W2
            stt(LR, A, 1.0, M, ALU.add, ALU.mult)
            tt(LR, LR, A, ALU.add)
            stt(LI, M, 1.0, B, ALU.add, ALU.mult)
            U, V, IN = sx[12][:], sx[13][:], sx[14][:]
            tt(U, lre, lre, ALU.mult)
            tt(V, lim, lim, ALU.mult)
            tt(U, U, V, ALU.add)
            ch.then(e.reciprocal(IN, U))
            tt(U, LR, lre, ALU.mult)
            tt(V, LI, lim, ALU.mult)
            tt(U, U, V, ALU.add)
            tt(pw[:, WR, :], U, IN, ALU.mult)
            tt(U, LI, lre, ALU.mult)
            tt(V, LR, lim, ALU.mult)
            tt(U, U, V, ALU.subtract)
            tt(pw[:, WI, :], U, IN, ALU.mult)
            ts(U, M, 1.0, None, ALU.add)
            tt(V, U, U, ALU.mult)
            tt(U, V, V, ALU.mult)
            tt(pw[:, RHO, :], U, U, ALU.mult)
            for _ in range(3):
                double()
            ts(pw[:, C8, :], A, 1.0, None, ALU.add)
            ts(pw[:, S8, :], B, 1.0, None, ALU.mult)
            ch.then(e.memset(pw[:, PR, :], 1.0))
            ch.then(e.memset(pw[:, PI, :], 0.0))
            ts(pw[:, PR + 1, :], LR, 1.0, None, ALU.add)
            ts(pw[:, PI + 1, :], LI, 1.0, None, ALU.mult)
            for k in range(2, CH + 1):
                r1, i1, r, i = pw[:, PR + 1, :], pw[:, PI + 1, :], pw[:, PR + k - 1, :], pw[:, PI + k - 1, :]
                tt(U, r, r1, ALU.mult)
                tt(V, i, i1, ALU.mult)
                tt(pw[:, PR + k, :], U, V, ALU.subtract)
                tt(U, r, i1, ALU.mult)
                tt(V, i, r1, ALU.mult)
                tt(pw[:, PI + k, :], U, V, ALU.add)
            e.memset(junk[:, 0:1], 0.0).then_inc(S("pw"), 1)
            e.wait_ge(S("c_t"), 1)
            e.tensor_scalar(cc[0][:], PS[:, 4, 0:SSM_W], sgn[:, 0:1], None, ALU.mult).then_inc(S("cc"), 1)
            e.tensor_scalar(cc[1][:], PS[:, 5, 0:SSM_W], -1.0, None, ALU.mult).then_inc(S("cc"), 1)
            ch.then(e.tensor_scalar(braw[1][:], braw[1][:], sgn[:, 1:2], None, ALU.mult))
            e.wait_ge(S("pw_t"), 1)
            for b in range(3):
                k = min(10, NQ - 10 * b)
                ch.then(e.tensor_copy(stn[:, 10 * b:10 * b + k, :], PS[:, 4 + b, 0:48 * k].rearrange("p (q n) -> p q n", n=48)))
            for k in range(CH + 1):
                ch.then(e.tensor_copy(stn[:, PRD + k, :], stn[:, PR + CH - k, :]))
                ch.then(e.tensor_copy(stn[:, PID + k, :], stn[:, PI + CH - k, :]))
            wr, wi = (stn[:, q, :].unsqueeze(2).to_broadcast([P, 2 * G, GC]) for q in (WR, WI))
            b1, b2 = (braw[i][:].rearrange("p d g c -> p (d g) c") for i in range(2))
            tt(btmp[0][:], b1, wr, ALU.mult)
            tt(btmp[1][:], b2, wi, ALU.mult)
            tt(bb[0][:], btmp[0][:], btmp[1][:], ALU.add)
            tt(btmp[0][:], b2, wr, ALU.mult)
            tt(btmp[1][:], b1, wi, ALU.mult)
            tt(bb[1][:], btmp[0][:], btmp[1][:], ALU.subtract)
            e.wait_ge(S("ada_mm"), 12)
            e.tensor_tensor(mod[:], PS[:, 7, 0:48], vec[:, VC["b_ada"]:VC["b_ada"] + 48], ALU.add).then_inc(S("mod"), 1)
            e.wait_ge(S("mod"), 1)
            for i, (v, g) in enumerate(((1, "g_pre_mix"), (4, "g_pre_ffn"))):
                e.scalar_tensor_tensor(gain1[:, i * 8:i * 8 + 8], mod[:, v * 8:v * 8 + 8], 1.0,
                                       vec[:, VC[g]:VC[g] + 8], ALU.add, ALU.mult).then_inc(S("mod"), 1)
            for i, (v, g) in enumerate(((2, "g_post_mix"), (5, "g_post_ffn"))):
                e.tensor_tensor(gain1[:, 16 + i * 8:24 + i * 8], mod[:, v * 8:v * 8 + 8], vec[:, VC[g]:VC[g] + 8],
                                ALU.mult).then_inc(S("mod"), 1)
            e.wait_ge(S("mod"), 5)
            e.tensor_scalar(bq[:], vec[:, VC["b_in"]:VC["b_in"] + 18], 0.125, None, ALU.mult).then_inc(S("gts"), 1)
            e.wait_ge(S("gr_t"), 1)
            e.tensor_copy(gr16[:], PS[0:16, 0, 0:P]).then_inc(S("gr"), 1)

        bq = at("bq", [P, 18], F32, R3 + 6720)
        gr16 = at("gr16", [16, P], F32, R3 + 6816)

        def prep_act_end(e):
            e.wait_ge(S("gr"), 1)
            e.dma_start(grow.rearrange("a (r c) -> (a r) c", c=P), gr16[:]).then_inc(S("gr_st"), 16)

        POST = [(post_m, grow[0], None, False), (post_f, grow[1], None, False),
                (post_f, t["ffn1_post_g_2"][0], None, True), (post_m, t["attn_post_g_2"][0], t["b_out_2"][0], False),
                (post_f, t["ffn2_post_g_2"][0], None, True), (post_m, t["ple_post_g_2"][0], "gate", False)]
        NORM = [(gain1[:, 0:8], mod[:, 0:8]), (gain1[:, 8:16], mod[:, 24:32])] + \
               [(vec[:, VC[n]:VC[n] + 8], None) for n in ("ffn1_pre", "attn_pre", "ffn2_pre", "ple_pre")]
        LAST = last - 1
        ys = lambda T: PSr[:, (T % 4) * D:(T % 4 + 1) * D]
        NG_G = [G_OUT1, G_DN[0], G_DN[1], G_OUT2, G_DN[2], [g + 4 for g in G_PLE]]
        NG_N = [4, 11, 11, 4, 11, 1]

        def wait_rows(e, p, T):
            grp, k = T // 4, T % 4
            if k < 3:
                e.wait_ge(S("ng_rdy"), (p * 2 + grp) * 3 + k + 1)
            else:
                e.wait_ge(S("w_used"), NG_G[p][grp] + NG_N[p])

        def n_loads(p):
            return sum(3 if POST[q][2] is not None and POST[q][2] != "gate" else 2 for q in range(p + 1))

        def post_load_act(e, p):
            b, g, bias, _ = POST[p]
            src = t["x"][0] if p == 0 else xs
            wait(e, S("x_st"), 16 * TT * p)
            if p < 2:
                e.wait_ge(S("gr_st"), 16)
            e.dma_start(b.x[:], src.rearrange("(t p) n -> p t n", p=P)).then_inc(S("x_ld"), 16)
            e.dma_start(b.g[:], g.partition_broadcast(P)).then_inc(S("x_ld"), 16)
            if bias is not None and bias != "gate":
                e.dma_start(b.bias[:], bias.partition_broadcast(P)).then_inc(S("x_ld"), 16)

        def post_sq_act(e, p, T):
            b, _, bias, half = POST[p]
            if bias is None:
                wait_rows(e, p, T)
                src = ys(T)
            else:
                e.wait_ge(S("n_y"), (p // 4) * 8 + T + 1)
                src = b.y[:]
            e.activation(act1[:], src, ACT.Square, accum_out=stat[:, 0, T:T + 1]).then_inc(S("n_sq"), 1)
            e.wait_ge(S("n_sq"), p * 8 + T + 1)
            s = 4.0 if half else 1.0
            e.activation(stat[:, 1, T:T + 1], stat[:, 0, T:T + 1], ACT.Sqrt, bias=epsc[:, 1:2] if half else epsc[:, 0:1],
                         scale=s / D).then_inc(S("n_rt"), 1)

        def post_dve(e, p, T):
            b, _, bias, _ = POST[p]
            e.wait_ge(S("x_ld"), 16 * n_loads(p))
            src = ys(T)
            if bias is not None:
                if bias == "gate":
                    e.wait_ge(S("gs"), T + 1)
                    wait_rows(e, p, T)
                    e.tensor_tensor(b.y[:], src, gs[:, T % 4, :], ALU.mult).then_inc(S("n_y"), 1)
                else:
                    wait_rows(e, p, T)
                    e.tensor_tensor(b.y[:], src, b.bias[:], ALU.add).then_inc(S("n_y"), 1)
                src = b.y[:]
            e.wait_ge(S("n_rt"), p * 8 + T + 1)
            e.reciprocal(stat[:, 2, T:T + 1], stat[:, 1, T:T + 1]).then_inc(S("n_r"), 1)
            e.wait_ge(S("n_r"), p * 8 + T + 1)
            e.scalar_tensor_tensor(b.tmp[:], src, stat[:, 2, T:T + 1], b.g[:], ALU.mult, ALU.mult)\
             .then_inc(S("n_tmp"), 1)
            e.wait_ge(S("n_tmp"), p * 8 + T + 1)
            e.tensor_tensor(b.x[:, T, :], b.x[:, T, :], b.tmp[:], ALU.add).then_inc(S("n_x"), 1)

        def post_store_act(e, p, T):
            e.wait_ge(S("n_x"), p * 8 + T + 1)
            dst = out[0] if p == LAST else xs
            e.dma_start(dst[T * P:(T + 1) * P, :], POST[p][0].x[:, T, :]).then_inc(S("x_st"), 16)

        def norm_rows(n):
            return xn if n == 0 else POST[n - 1][0].x

        def norm_sq_act(e, n, T):
            if n == 0:
                e.wait_ge(S("x0_ld"), 16)
                e.wait_ge(S("eps"), 2)
            else:
                e.wait_ge(S("n_x"), (n - 1) * 8 + T + 1)
            e.activation(act1[:], norm_rows(n)[:, T, :], ACT.Square, accum_out=stat[:, 3, T:T + 1]).then_inc(S("m_sq"), 1)
            e.wait_ge(S("m_sq"), n * 8 + T + 1)
            e.activation(stat[:, 4, T:T + 1], stat[:, 3, T:T + 1], ACT.Sqrt, bias=epsc[:, 0:1], scale=1.0 / D)\
             .then_inc(S("m_rt"), 1)

        def norm_r_dve(e, n, T):
            e.wait_ge(S("m_rt"), n * 8 + T + 1)
            e.reciprocal(stat[:, 5, T:T + 1], stat[:, 4, T:T + 1]).then_inc(S("m_r"), 1)

        def norm_scale_act(e, n, T):
            e.wait_ge(S("m_r"), n * 8 + T + 1)
            e.activation(xn[:, T, :], norm_rows(n)[:, T, :], ACT.Copy, scale=stat[:, 5, T:T + 1]).then_inc(S("m_xn"), 1)

        def norm_pe(e, n):
            for hf in range(2):
                e.wait_ge(S("m_xn"), n * 8 + (hf + 1) * 4)
                if n > 0:
                    e.wait_ge(S("n_tmp"), n * 8 - 3 if hf == 0 else n * 8)
                for k in range(KT):
                    q = n * 16 + hf * KT + k
                    wait(e, S("ht_f"), q - 1)
                    for i in range(4):
                        mm = e.transpose(PS[:, k % 2, i * P:(i + 1) * P], xn[:, hf * 4 + i, k * P:(k + 1) * P], ident[:])
                    mm.then_inc(S("ht_t"), 1)

        def norm_out_act(e, n):
            g, s = NORM[n]
            if n == 0:
                e.wait_ge(S("mod"), 5)
            for q in range(16):
                k = q % KT
                e.wait_ge(S("ht_t"), n * 16 + q + 1)
                wait(e, S("ht_lo"), n * 16 + q - 1)
                e.activation(fold[q % 2][:], PS[:, k % 2, :], ACT.Identity, scale=g[:, k:k + 1],
                             bias=0.0 if s is None else s[:, k:k + 1]).then_inc(S("ht_f"), 1)

        def norm_out_dve(e, n):
            if n == 0:
                e.wait_ge(S("tb_st0"), 128)
                e.wait_ge(S("tb_st1"), 128)
            else:
                e.wait_ge(S("x_st"), 16 * TT * n)
            for q in range(16):
                k, hf = q % KT, q // KT
                e.wait_ge(S("ht_f"), n * 16 + q + 1)
                o = (slice(None), k, slice(hf * 512, hf * 512 + 512))
                e.tensor_copy(h_hi[o], fold[q % 2][:]).then_inc(S("ht_hi"), 1)
                e.wait_ge(S("ht_hi"), n * 16 + q + 1)
                e.tensor_tensor(h_lo[o], fold[q % 2][:], h_hi[o].bitcast(F32), ALU.subtract).then_inc(S("ht_lo"), 1)

        def three(e, outs, a, bs, start, stop):
            for ai, bi, first, end in ((0, 0, True, False), (0, 1, False, False), (1, 0, False, True)):
                for o, b in zip(outs, bs):
                    mm = e.matmul(o, a[ai], b[bi], start=start and first, stop=stop and end)
            return mm

        def rows_chunk_pe(e, g, b, lhs, free, first, end, p):
            e.wait_ge(S("w_split"), g + 1)
            wh, wl = w_view(b, "rows", "hi"), w_view(b, "rows", "lo")
            for i in range(4):
                if first and free is not None:
                    e.wait_ge(S(free[0]), free[1] + i + 1)
                for kk in range(2):
                    mm = three(e, [PS[:, 2 * i + h, :] for h in range(2)], lhs(kk, i),
                               [(wh[:, kk, h * 512:(h + 1) * 512], wl[:, kk, h * 512:(h + 1) * 512]) for h in range(2)],
                               first and kk == 0, end and kk == 1)
                if end and i < 3 and p is not None:
                    mm.then_inc(S("ng_rdy") if p >= 0 else S("gate_rdy"), 1)
            mm.then_inc(S("w_used"), 1)

        def from_tiles(hi, lo, k0, grp):
            return lambda kk, i: tuple(v[:, k0 + kk, (grp * 4 + i) * P:(grp * 4 + i + 1) * P] for v in (hi, lo))

        def out_pe(e, p):
            e.wait_ge(S("at_yl"), 6 if p == 0 else 22)
            e.wait_ge(S("at_o"), 48 if p == 0 else 176)
            if p == 0:
                e.wait_ge(S("gl_l"), 3)
                e.wait_ge(S("gl_h"), 3)
            for grp in range(2):
                for m in range(4):
                    g = NG_G[p][grp] + m
                    rows_chunk_pe(e, g, g % NBUF, from_tiles(y_hi, y_lo, 2 * m, grp),
                                  ("n_tmp", p * 8) if grp else None,
                                  m == 0, m == 3, p)

        def down_pe(e, p):
            for grp in range(2):
                g0 = NG_G[p][grp]
                s0 = DN_S[p] + grp * 11

                def chunk(g, m, j0, first, end):
                    b = (s0 + j0) % 3
                    e.wait_ge(S("a_split"), s0 + 1 + m)
                    lhs = lambda kk, i: (a_hi[b][:, kk, i * P:(i + 1) * P], a_lo[b][:, kk, i * P:(i + 1) * P])
                    rows_chunk_pe(e, g, (g0 + j0) % NBUF, lhs, ("n_tmp", p * 8) if grp else None, first, end, p)

                chunk(g0, 0, 0, True, False)
                repeat(e, 9, 3, lambda i, j, turn: chunk(i + (g0 + 1), i + 1, 1 + j, False, False))
                chunk(g0 + 10, 10, 10, False, True)

        DN_S = {1: 0, 2: 22, 4: 44}

        def split_a(e, p, grp, m, j0, act):
            s0 = DN_S[p] + grp * 11
            b = (s0 + j0) % 3
            src = aT[:].rearrange("p (m k) n -> p m k n", k=2)[:, ds(m, 1), :, grp * 512:(grp + 1) * 512]\
                .rearrange("p o k n -> p (o k) n")
            if act:
                g = NG_G[p][grp] + m
                wait_alone(e, S("w_used"), g - 2, S("idc"))
                e.activation(a_hi[b][:], src, ACT.Copy).then_inc(S("a_hi"), 1)
            else:
                e.wait_ge(S("a_hi"), s0 + 1 + m)
                e.tensor_tensor(a_lo[b][:], src, a_hi[b][:].bitcast(F32), ALU.subtract).then_inc(S("a_split"), 1)

        def down_act(e, p):
            e.wait_ge(S("w_used"), NG_G[p][0])
            e.wait_ge(S("f_out"), 2 + FT * (F_OF[p] + 1))
            post_load_act(e, p)
            split_a(e, p, 0, 0, 0, True)
            split_a(e, p, 0, 1, 1, True)
            repeat(e, 9, 3, lambda i, j, turn: split_a(e, p, 0, i + 2, 2 + j, True))
            for m in range(2):
                split_a(e, p, 1, m, m, True)
            for T in range(4):
                post_sq_act(e, p, T)
            split_a(e, p, 1, 2, 2, True)
            for T in range(4):
                post_store_act(e, p, T)
                if p != LAST:
                    norm_sq_act(e, p + 1, T)
            split_a(e, p, 1, 3, 3, True)
            split_a(e, p, 1, 4, 4, True)
            repeat(e, 6, 3, lambda i, j, turn: split_a(e, p, 1, i + 5, 5 + j, True))
            tail_act(e, p, range(4, 8))

        def down_dve(e, p):
            split_a(e, p, 0, 0, 0, False)
            split_a(e, p, 0, 1, 1, False)
            repeat(e, 9, 3, lambda i, j, turn: split_a(e, p, 0, i + 2, 2 + j, False))
            for m in range(2):
                split_a(e, p, 1, m, m, False)
            for T in range(4):
                post_dve(e, p, T)
            split_a(e, p, 1, 2, 2, False)
            if p != LAST:
                for T in range(4):
                    norm_r_dve(e, p + 1, T)
            split_a(e, p, 1, 3, 3, False)
            split_a(e, p, 1, 4, 4, False)
            repeat(e, 6, 3, lambda i, j, turn: split_a(e, p, 1, i + 5, 5 + j, False))
            tail_dve(e, p, range(4, 8))

        F_OF = {1: 0, 2: 1, 4: 2}

        def tail_act(e, p, tiles):
            for T in tiles:
                post_sq_act(e, p, T)
                if T > tiles[0]:
                    post_store_act(e, p, T - 1)
                    if p != LAST:
                        norm_sq_act(e, p + 1, T - 1)
            post_store_act(e, p, tiles[-1])
            if p == LAST:
                return
            norm_sq_act(e, p + 1, tiles[-1])
            for T in range(TT):
                norm_scale_act(e, p + 1, T)
            norm_out_act(e, p + 1)

        def tail_dve(e, p, tiles):
            for T in tiles:
                post_dve(e, p, T)
                if T > tiles[0] and p != LAST:
                    norm_r_dve(e, p + 1, T - 1)
            if p != LAST:
                norm_r_dve(e, p + 1, tiles[-1])
                norm_out_dve(e, p + 1)

        def out_act(e, p):
            e.wait_ge(S("at_o"), 48 if p == 0 else 176)
            post_load_act(e, p)
            for T in range(4):
                post_sq_act(e, p, T)
            for T in range(4):
                post_store_act(e, p, T)
                if p != LAST:
                    norm_sq_act(e, p + 1, T)
            tail_act(e, p, range(4, 8))

        def out_dve(e, p):
            for T in range(4):
                post_dve(e, p, T)
            if p != LAST:
                for T in range(4):
                    norm_r_dve(e, p + 1, T)
            tail_dve(e, p, range(4, 8))

        def up_pe(e, f):
            g0 = G_UP[f]
            e.wait_ge(S("ht_lo"), 16 * (NORM_OF[f] + 1))

            def chunk(i, j, turn):
                b = (g0 + j) % NBUF
                e.wait_ge(S("w_split"), i + (g0 + 1))
                e.wait_ge(S("f_out"), i + (1 + FT * f))
                wh, wl = w_view(b, "cols", "hi"), w_view(b, "cols", "lo")
                o = 4 * (j % 2)
                for m in range(2):
                    for k in range(KT):
                        mm = three(e, [PS[:, o + 2 * m + h, :] for h in range(2)],
                                   (wh[:, k, m * P:(m + 1) * P], wl[:, k, m * P:(m + 1) * P]),
                                   [(h_hi[:, k, h * 512:(h + 1) * 512], h_lo[:, k, h * 512:(h + 1) * 512]) for h in range(2)],
                                   k == 0, k == KT - 1)
                mm.then_inc(S("w_used"), 1)

            repeat(e, FT, 6, chunk)

        NORM_OF = [1, 2, 4]

        def up_act(e, f):
            def chunk(i, j, turn):
                o = 4 * (j % 2)
                gate, val = PSr[:, o * 512:(o + 2) * 512], PSr[:, (o + 2) * 512:(o + 4) * 512]
                e.wait_ge(S("w_used"), i + (G_UP[f] + 1))
                wait_alone(e, S("f_out"), i + (2 + FT * f), S("idc"))
                if f:
                    e.activation(act1[:], gate, ACT.Silu).then_inc(S("f_act"), 1)
                    return
                one = lambda c: vec[:, ds(i + c, 1)]
                e.activation(act1[:], gate, ACT.Identity, scale=one(VC["conv_w"] + 2 * FT), bias=one(VC["conv_b"]))\
                 .then_inc(S("f_act"), 1)
                e.activation(aT[:, ds(i, 1), :].rearrange("p o n -> p (o n)"), val, ACT.Identity,
                             scale=one(VC["conv_w"] + 3 * FT), bias=one(VC["conv_b"] + FT)).then_inc(S("f_act"), 1)
                e.wait_ge(S("f_tap"), i * 4 + 2)
                e.activation(act1[:], act1[:], ACT.Gelu_apprx_tanh).then_inc(S("f_gelu"), 1)

            repeat(e, FT, 6, chunk)

        def up_dve(e, f):
            def chunk(i, j, turn):
                o = 4 * (j % 2)
                gate, val = PSr[:, o * 512:(o + 2) * 512], PSr[:, (o + 2) * 512:(o + 4) * 512]
                a = aT[:, ds(i, 1), :].rearrange("p o n -> p (o n)")
                if f:
                    e.wait_ge(S("f_act"), i + (2 * FT + 1 + FT * (f - 1)))
                    e.tensor_tensor(a, act1[:], val, ALU.mult).then_inc(S("f_out"), 1)
                    return
                for c, (dst, src) in enumerate(((act1[:], gate), (a, val))):
                    e.wait_ge(S("f_act"), i * 2 + (c + 1))
                    one = lambda tap: vec[:, ds(i + (VC["conv_w"] + (2 * tap + c) * FT), 1)]
                    e.scalar_tensor_tensor(dst[:, 1:], src[:, 0:SEQ - 1], one(0), dst[:, 1:], ALU.mult, ALU.add)\
                     .then_inc(S("f_tap"), 1)
                    e.wait_ge(S("f_tap"), i * 4 + (2 * c + 1))
                    e.scalar_tensor_tensor(dst[:, 0:SEQ - 1], src[:, 1:], one(2), dst[:, 0:SEQ - 1], ALU.mult, ALU.add)\
                     .then_inc(S("f_tap"), 1)
                e.wait_ge(S("f_gelu"), i + 1)
                e.wait_ge(S("f_tap"), i * 4 + 4)
                e.tensor_tensor(a, act1[:], a, ALU.mult).then_inc(S("f_out"), 1)

            repeat(e, FT, 6, chunk)

        u_nat = at("u_nat", [P, CH, SSM_W], F32, 32 * KB)
        fT = at("fT", [P, 2, SEQ], F32, 44 * KB)
        zst = [at(f"zst{i}", [P, SEQ], F32, 52 * KB + i * 4 * KB) for i in range(2)]
        vbias = at("vbias", [P, 640], F32, 60 * KB)
        Z1 = [(0, "u", 0, 256, 0, 4, 0), (0, "u", 0, 256, 4, 4, 0), (1, "u", 0, P, 0, 8, 256), (1, "f", P, P, 0, 0, 0),
              (2, "f", 0, P, 0, 0, 1), (2, "q", P, P, 0, 0, 0), (3, "q", 0, P, 0, 0, 1), (3, "q", P, P, 0, 0, 2),
              (4, "k", 0, P, 0, 0, 3), (4, "v", P, P, 0, 8, 0)]
        Z2 = [(0, "q", 0, P, 0, 0, 0), (0, "q", P, P, 0, 0, 1), (1, "q", 0, P, 0, 0, 2), (1, "q", P, P, 0, 0, 3),
              (2, "k", 0, P, 0, 0, 4), (2, "v", P, P, 0, 8, 0)]
        Z2 += [(3 + r // 2, "q" if r < 4 else "k", r % 2 * P, P, 0, 0, 5 + r) for r in range(8)]
        Z2 += [(7 + c, "v", 0, 256, 4 * h, 4, P + 256 * c) for c in range(2) for h in range(2)]
        ZS = [(Z1, G_Z1), (Z2, G_Z2)]

        def z_slots(z):
            slots, _ = ZS[z]
            inner, stores = 0, [0, 0]
            if z:
                inner = sum(1 for w, s in enumerate(Z1) if not (w + 1 == len(Z1) or Z1[w + 1][0] != s[0]))
                for w, s in enumerate(Z1):
                    stores[w % 2] += s[1] in "qkv"
            for w, s in enumerate(slots):
                end = w + 1 == len(slots) or slots[w + 1][0] != s[0]
                yield w, s, end, inner, tuple(stores)
                inner += not end
                stores[w % 2] += s[1] in "qkv"

        def z_pe(e, z):
            slots, g0 = ZS[z]
            e.wait_ge(S("ht_lo"), 16 * (1 if z == 0 else 4))
            base = 0 if z == 0 else len(Z1)
            for w, (c, kind, c0, width, t0, nt, _), end, _, _ in z_slots(z):
                g = g0 + c
                b = g % NBUF
                o = w % 4 * SEQ
                e.wait_ge(S("w_split"), g + 1)
                if w >= 4:
                    e.wait_ge(S("z_ev"), base + w - 3)
                wh, wl = w_view(b, "cols", "hi"), w_view(b, "cols", "lo")
                cs = slice(c0, c0 + width)
                if nt == 0:
                    for k in range(KT):
                        mm = three(e, [PSr[:, o + h * 512:o + h * 512 + 512] for h in range(2)], (wh[:, k, cs], wl[:, k, cs]),
                                   [(h_hi[:, k, h * 512:(h + 1) * 512], h_lo[:, k, h * 512:(h + 1) * 512]) for h in range(2)],
                                   k == 0, k == KT - 1)
                else:
                    for i in range(nt):
                        T = t0 + i
                        pos = slice(T, SEQ, CH) if kind == "u" else slice(T * P, (T + 1) * P)
                        for k in range(KT):
                            mm = three(e, [PSr[:, o + i * width:o + (i + 1) * width]], (h_hi[:, k, pos], h_lo[:, k, pos]),
                                       [(wh[:, k, cs], wl[:, k, cs])], k == 0, k == KT - 1)
                mm.then_inc(S("w_used") if end else S("z_rdy"), 1)

        def z_wait(e, z, c, end, inner):
            if end:
                e.wait_ge(S("w_used"), ZS[z][1] + c + 1)
            else:
                e.wait_ge(S("z_rdy"), inner + 1)

        def z_act(e, z):
            base = 0 if z == 0 else len(Z1)
            if z:
                e.dma_start(vbias[:, 0:P], t["b_in_2"][0, 640:768].partition_broadcast(P)).then_inc(S("vb_ld"), 16)
                e.dma_start(vbias[:, P:640], t["b_in_2"][0, 1792:2304].partition_broadcast(P)).then_inc(S("vb_ld"), 16)
            for w, (c, kind, c0, width, t0, nt, to), end, inner, stores in z_slots(z):
                src = PSr[:, w % 4 * SEQ:(w % 4 + 1) * SEQ]
                st = zst[w % 2]
                if z and kind == "v":
                    e.wait_ge(S("z_ev"), base + w + 1)
                else:
                    z_wait(e, z, c, end, inner)
                    if kind in "qkv":
                        wait(e, S(f"z_st{w % 2}"), 16 * stores[w % 2])
                    if kind == "u":
                        e.activation(u_nat[:, t0:t0 + nt, to:to + width], src.rearrange("p (t n) -> p t n", t=nt), ACT.Copy)\
                         .then_inc(S("z_ev"), 1)
                    elif kind == "f":
                        e.activation(fT[:, to, :], src, ACT.Copy).then_inc(S("z_ev"), 1)
                    elif kind == "v":
                        e.activation(st[:], src, ACT.Copy).then_inc(S("z_ev"), 1)
                    else:
                        col = to if to < 5 else to + 1
                        scale = 0.125 if kind == "q" else 1.0
                        bias = 0.0 if z == 0 else bq[:, col:col + 1] if kind == "q" else vcol("b_in", col)
                        e.activation(st[:], src, ACT.Identity, scale=scale, bias=bias).then_inc(S("z_ev"), 1)
                    e.wait_ge(S("z_ev"), base + w + 1)
                if kind in "qk":
                    e.dma_start(qk[to * P:(to + 1) * P, :], st[:]).then_inc(S(f"z_st{w % 2}"), 16)
                elif kind == "v":
                    e.dma_start(vs.rearrange("(t p) n -> p t n", p=P)[:, t0:t0 + nt, to:to + width],
                                st[:].rearrange("p (t n) -> p t n", t=nt)).then_inc(S(f"z_st{w % 2}"), 16)

        def z_dve(e, z):
            if z == 0:
                return
            e.wait_ge(S("vb_ld"), 32)
            for w, (c, kind, c0, width, t0, nt, to), end, inner, stores in z_slots(z):
                if kind != "v":
                    continue
                z_wait(e, z, c, end, inner)
                wait(e, S(f"z_st{w % 2}"), 16 * stores[w % 2])
                e.wait_ge(S("z_ev"), len(Z1) + w)
                e.tensor_tensor(zst[w % 2][:].rearrange("p (t n) -> p t n", t=nt),
                                PSr[:, w % 4 * SEQ:(w % 4 + 1) * SEQ].rearrange("p (t n) -> p t n", t=nt),
                                vbias[:, to:to + width].unsqueeze(1).to_broadcast([P, nt, width]), ALU.add)\
                 .then_inc(S("z_ev"), 1)

        def z_stores(z, par):
            return 16 * sum(1 for q in range(z + 1) for w, s in enumerate(ZS[q][0]) if w % 2 == par and s[1] in "qkv")

        cd = at("cd", [P, 2, P], F32, 60 * KB)
        wf = at("wf", [P, 2, HD], F32, 61 * KB)
        bd = at("bd", [P, 2, 2, P], F32, 62 * KB)
        fp_hi = at("fp_hi", [P, TT, 2, 2 * P], F32R, R1 + 16 * KB)
        fp_lo = at("fp_lo", [P, TT, 2, 2 * P], F32R, R1 + 48 * KB)

        def fft_loads(e):
            e.dma_start(cd[:], t["dft_head"]).then_inc(S("ff_ld"), 16)
            e.dma_start(wf[:], t["w_fft"][0].rearrange("(a h) d e -> (h d) a e", h=2)).then_inc(S("ff_ld"), 16)

        def fft_pe(e):
            e.wait_ge(S("ff_ld"), 32)
            e.wait_ge(S("z_ev"), len(Z1))
            for a in range(2):
                for c in range(2):
                    mm = e.matmul(PS[:, 0, (a * 2 + c) * HD:(a * 2 + c + 1) * HD], cd[:, c, :], wf[:, a, :], start=True, stop=True)
            mm.then_inc(S("ff_w"), 1)
            e.wait_ge(S("ff_bd"), 9)
            for T in range(TT):
                if T >= 4:
                    e.wait_ge(S("ff_lo"), T - 3)
                for a in range(2):
                    mm = e.matmul(PS[:, 4 + T % 4, a * 256:(a + 1) * 256], fT[:, a, T * P:(T + 1) * P],
                                  bd[:, a, :, :].rearrange("p c n -> p (c n)"), start=True, stop=True)
                mm.then_inc(S("ff_p"), 1)
            e.wait_ge(S("ff_lo"), TT)
            for kt in range(TT):
                g = G_DFT + kt
                b = g % NBUF
                e.wait_ge(S("w_split"), g + 1)
                wh, wl = w_view(b, "rows", "hi"), w_view(b, "rows", "lo")
                for a in range(2):
                    for c in range(2):
                        cs = slice(c * P, (c + 1) * P)
                        mm = three(e, [PS[:, 2 * a + h, :] for h in range(2)], (fp_hi[:, kt, a, cs], fp_lo[:, kt, a, cs]),
                                   [(wh[:, c, h * 512:(h + 1) * 512], wl[:, c, h * 512:(h + 1) * 512]) for h in range(2)],
                                   kt == 0 and c == 0, kt == TT - 1 and c == 1)
                mm.then_inc(S("w_used"), 1)

        def fft_act(e):
            e.wait_ge(S("ff_bd"), 1)
            e.wait_ge(S("ff_w"), 1)
            for a in range(2):
                for c in range(2):
                    for h in range(2):
                        r = slice(h * HD, (h + 1) * HD)
                        e.activation(bd[r, a, c, h * HD:(h + 1) * HD], PS[r, 0, (a * 2 + c) * HD:(a * 2 + c + 1) * HD],
                                     ACT.Copy, scale=1.0 / 256).then_inc(S("ff_bd"), 1)
            for T in range(TT):
                e.wait_ge(S("ff_p"), T + 1)
                if T == 0:
                    e.wait_ge(S("w_used"), G_Z1 + 5)
                e.activation(fp_hi[:, T, :, :].rearrange("p a n -> p (a n)"), PS[:, 4 + T % 4, :], ACT.Copy).then_inc(S("ff_hi"), 1)
            e.wait_ge(S("w_used"), G_DFT + TT)
            e.activation(y_hi[:, 3:5, :].rearrange("p a n -> p (a n)"), PSr[:, 0:2 * SEQ], ACT.Copy).then_inc(S("ff_y"), 1)

        def fft_dve(e):
            e.memset(bd[:], 0.0).then_inc(S("ff_bd"), 1)
            for T in range(TT):
                e.wait_ge(S("ff_hi"), T + 1)
                e.tensor_tensor(fp_lo[:, T, :, :].rearrange("p a n -> p (a n)"), PS[:, 4 + T % 4, :],
                                fp_hi[:, T, :, :].rearrange("p a n -> p (a n)").bitcast(F32), ALU.subtract).then_inc(S("ff_lo"), 1)
            e.wait_ge(S("ff_y"), 1)
            e.tensor_tensor(y_lo[:, 3:5, :].rearrange("p a n -> p (a n)"), PSr[:, 0:2 * SEQ],
                            y_hi[:, 3:5, :].rearrange("p a n -> p (a n)").bitcast(F32), ALU.subtract).then_inc(S("ff_y2"), 1)

        q1 = GSUB * P
        y_nat = at("y_nat", [P, CH, SSM_W], F32, 0)
        yT = at("yT", [P, 3, SEQ], F32, 12 * KB)
        ug = at("ug", [P, GSUB, CH, GC], F32, 24 * KB)
        uT = at("uT", [P, GSUB, P], F32, 26 * KB)
        mm_ = at("mm_", [P, GSUB, P], F32, 28 * KB)
        b1s = at("b1s", [P, 2, GSUB, GC], F32, 30 * KB)
        drow = at("drow", [P, SSM_W], F32, 82 * KB)
        gT = at("gT", [P, 2, 2, GSUB, P], F32, R1)
        av = at("av", [P, 2, 2, GSUB, P], F32, R1 + 20 * KB)
        cosn = at("cosn", [P, 2 * GSUB, P], F32, R1 + 8 * KB)
        sinn = at("sinn", [P, 2 * GSUB, P], F32, R1 + 28 * KB)
        gs_ = at("gs_", [P, 2, 2, GSUB, P], F32, R1 + 32 * KB)
        t1 = at("t1", [P, 2 * GSUB, P], F32, R1 + 40 * KB)
        t2 = at("t2", [P, 2 * GSUB, P], F32, R1 + 52 * KB)
        gt = [at(f"gt{i}", [P, GSUB, CH, GC], F32, R1 + 56 * KB + i * 2 * KB) for i in range(2)]
        rt = [at(f"rt{i}", [P, 2 * GSUB, HD], F32, R1 + 60 * KB + i * 2 * KB) for i in range(2)]
        rf = at("rf", [P, 2, 8, 2 * GSUB], F32, 31 * KB)
        rft = at("rft", [P, 2, 2 * GSUB], F32, 31 * KB + 512)
        oo = [at(f"oo{i}", [P, 2, GSUB, 9, GC], F32, 44 * KB + i * 5 * KB) for i in range(2)]
        ot = [at(f"ot{i}", [P, GSUB, 9, GC], F32, 54 * KB + i * 2560) for i in range(2)]
        ksb = at("ksb", [GC, GSUB, 256], F32, 59 * KB)
        TURNS = G // GSUB
        ND, NPL = 12 + 4 + 8 + 4 + 1, 12 + 2 + 6 * 5 + 2 + 7 * 6
        st4 = lambda q, n, d, g0: stn[:].rearrange("p q (d g) -> p q d g", d=2)[:, q:q + n, d, ds(g0, GSUB)]

        def ssm_turns(e, body):
            body(0, 0, 0)
            repeat(e, TURNS - 1, 1, lambda i, j, turn: body(i + 1, 0, i + 1))

        def ssm_act(e):
            e.dma_start(drow[:], t["d_skip"][0].partition_broadcast(P)).then_inc(S("ss_ld"), 16)

            def turn_(i, j, turn):
                g0 = i * GSUB
                wait(e, S("ss_ut"), i)
                e.activation(ug[:].rearrange("p g t c -> p t g c"),
                             u_nat[:].rearrange("p t (g c) -> p t g c", c=GC)[:, :, ds(g0, GSUB), :], ACT.Copy)\
                 .then_inc(S("ss_ug"), 1)
                wait(e, S("ss_k"), i)
                e.activation(b1s[:], bb[0][:].rearrange("p (d g) c -> p d g c", d=2)[:, :, ds(g0, GSUB), :], ACT.Copy)\
                 .then_inc(S("ss_b1"), 1)
                e.wait_ge(S("ss_ut"), i + 1)
                wait(e, S("ss_y"), i)
                e.activation(uT[:].rearrange("p g n -> p (g n)"), PS[:, 0, :], ACT.Copy).then_inc(S("ss_uc"), 1)
                for h in range(2):
                    e.wait_ge(S("ss_gp"), i * 2 + (h + 1))
                    e.activation(gT[:, h].rearrange("p d g n -> p (d g n)"), PSr[:, (2 + h) * SEQ:(3 + h) * SEQ], ACT.Copy)\
                     .then_inc(S("ss_gt"), 1)
                e.wait_ge(S("ss_k"), i + 1)
                wait(e, S("kd"), i * 16)
                e.activation(ksb[:, :, 0:240], PS[0:GC, 1:3, :].rearrange("p b (g n) -> p (b g) n", n=256)[:, :, 0:240],
                             ACT.Copy).then_inc(S("ss_kc"), 1)

            ssm_turns(e, turn_)
            e.wait_ge(S("ssd"), 1 + ND * TURNS + 1)
            e.activation(y_nat[:].rearrange("p t c -> p (t c)"), y_nat[:].rearrange("p t c -> p (t c)"),
                         ACT.Gelu_apprx_tanh).then_inc(S("ss_gl"), 1)
            for m in range(3):
                for h in range(2):
                    q = m * 2 + h
                    e.wait_ge(S("ss_yt"), q + 1)
                    src = PS[:, q % 2, :].rearrange("p (t n) -> p n t", t=4)
                    dst = yT[:, m, :].rearrange("p (n t) -> p n t", t=CH)[:, :, h * 4:h * 4 + 4]
                    e.activation(dst, src, ACT.Copy).then_inc(S("ss_ye"), 1)
                e.wait_ge(S("ss_ye"), 2 * m + 2)
                e.activation(y_hi[:, m, :], yT[:, m, :], ACT.Copy).then_inc(S("ss_yh"), 1)
            for m in range(3):
                if m == 2:
                    e.wait_ge(S("w_used"), G_GLU + 1)
                else:
                    e.wait_ge(S("gl_mm"), m + 1)
                e.activation(sig[:, m, :], PSr[:, (m + 1) * SEQ:(m + 2) * SEQ], ACT.Sigmoid).then_inc(S("gl_s"), 1)
            for m in range(3):
                e.wait_ge(S("gl_y"), m + 1)
                e.activation(y_hi[:, m, :], yT[:, m, :], ACT.Copy).then_inc(S("gl_h"), 1)

        sig = at("sig", [P, 3, SEQ], F32, 44 * KB)

        def ssm_sp(e):
            def turn_(i, j, turn):
                wait_alone(e, S("ss_kc"), i + 1, S("idc"))
                e.dma_start(kpd.rearrange("g c n -> c g n"), ksb[:, :, 0:240]).then_inc(S("kd"), 16)
                wait_alone(e, S("kd"), i * 16 + 16, S("idc"))
                wait_alone(e, S("ss_y"), i, S("idc"))
                for s in range(CH):
                    e.dma_start(mm_[s * GC:(s + 1) * GC, :, :],
                                kpd.rearrange("g c n -> c g n")[:, :, (7 - s) * GC:(7 - s) * GC + P]).then_inc(S("km"), 16)
                wait_alone(e, S("km"), i * 128 + 128, S("idc"))
            ssm_turns(e, turn_)

        def ssm_pool(e):
            def turn_(i, j, turn):
                g0 = i * GSUB
                ch = Chain(e, S("ssp"), i * NPL, S("idc"))
                wait_alone(e, S("ss_gp"), i * 2, S("idc"))
                e.wait_ge(S("ff_y2"), 1)
                for d in range(2):
                    qr, qi = (PRD + 1, PID + 1) if d == 0 else (PR, PI)
                    r, m = (st4(q, CH, d, g0).rearrange("p t g -> p g t").unsqueeze(3).to_broadcast([P, GSUB, CH, GC])
                            for q in (qr, qi))
                    b1, b2 = (bb[k][:].rearrange("p (d g) c -> p d g c", d=2)[:, d, ds(g0, GSUB), :]
                              .unsqueeze(2).to_broadcast([P, GSUB, CH, GC]) for k in range(2))
                    g4 = [gs_[:, k, d].rearrange("p g (t c) -> p g t c", c=GC) for k in range(2)]
                    for k, (x0, x1, op) in enumerate((((r, b1), (m, b2), ALU.add), ((m, b1), (r, b2), ALU.subtract))):
                        for y, (a, b) in enumerate((x0, x1)):
                            ch.then(e.tensor_tensor(gt[y][:], a, b, ALU.mult))
                        ch.then(e.tensor_tensor(g4[k], gt[0][:], gt[1][:], op))
                wait_alone(e, S("ssd"), i * ND + 1, S("idc"))
                c8, s8 = (stn[:].rearrange("p q (d g) -> p q d g", d=2)[:, q, :, ds(g0, GSUB)] for q in (C8, S8))
                ch.then(e.tensor_copy(rf[:, 0, 0, :].rearrange("p (d g) -> p d g", d=2), c8))
                ch.then(e.tensor_copy(rf[:, 1, 0, :].rearrange("p (d g) -> p d g", d=2), s8))
                for k in range(6):
                    c, s = rf[:, 0, k, :], rf[:, 1, k, :]
                    ch.then(e.tensor_tensor(rft[:, 0, :], s, s, ALU.mult))
                    ch.then(e.tensor_tensor(rft[:, 1, :], c, s, ALU.mult))
                    ch.then(e.tensor_tensor(rf[:, 0, k + 1, :], c, c, ALU.mult))
                    ch.then(e.tensor_tensor(rf[:, 0, k + 1, :], rf[:, 0, k + 1, :], rft[:, 0, :], ALU.subtract))
                    ch.then(e.tensor_tensor(rf[:, 1, k + 1, :], rft[:, 1, :], rft[:, 1, :], ALU.add))
                ch.then(e.memset(cosn[:, :, 0:1], 1.0))
                ch.then(e.memset(sinn[:, :, 0:1], 0.0))
                for k in range(7):
                    w = 1 << k
                    lo, hi = slice(0, w), slice(w, 2 * w)
                    c, s = (rf[:, x, k, :].unsqueeze(2).to_broadcast([P, 2 * GSUB, w]) for x in range(2))
                    a, b = rt[0][:, :, 0:w], rt[1][:, :, 0:w]
                    ch.then(e.tensor_tensor(a, cosn[:, :, lo], c, ALU.mult))
                    ch.then(e.tensor_tensor(b, sinn[:, :, lo], s, ALU.mult))
                    ch.then(e.tensor_tensor(cosn[:, :, hi], a, b, ALU.subtract))
                    ch.then(e.tensor_tensor(a, cosn[:, :, lo], s, ALU.mult))
                    ch.then(e.tensor_tensor(b, sinn[:, :, lo], c, ALU.mult))
                    ch.then(e.tensor_tensor(sinn[:, :, hi], a, b, ALU.add))
                assert ch.n == NPL, ch.n
            ssm_turns(e, turn_)

        def ssm_pe(e):
            e.wait_ge(S("ff_y2"), 1)

            def turn_(i, j, turn):
                e.wait_ge(S("ss_ug"), i + 1)
                wait(e, S("ss_uc"), i)
                for g in range(GSUB):
                    mm = e.transpose(PS[:, 0, g * P:(g + 1) * P], ug[:, g].rearrange("p t c -> p (t c)"), ident[:])
                mm.then_inc(S("ss_ut"), 1)
                e.wait_ge(S("ss_b1"), i + 1)
                wait(e, S("ss_kc"), i)
                e.wait_ge(S("ssd"), i * ND + 13)
                for g in range(GSUB):
                    o = PS[0:GC, 1 + g // 2, (g % 2) * 256:(g % 2) * 256 + 240]
                    e.matmul(o[:, 112:240], b1s[:, 0, g, :], oo[0][:, 0, g, 0:CH, :].rearrange("p t c -> p (t c)"),
                             start=True, stop=False, skip_group_check=True)
                    mm = e.matmul(o[:, 0:P], b1s[:, 1, g, :], oo[0][:, 1, g, 1:9, :].rearrange("p t c -> p (t c)"),
                                  start=False, stop=True, skip_group_check=True)
                mm.then_inc(S("ss_k"), 1)
                e.wait_ge(S("ssp"), i * NPL + 12)
                wait(e, S("ssd"), i * ND + 1)
                for h in range(2):
                    for u in range(2 * GSUB):
                        mm = e.transpose(PSr[:, (2 + h) * SEQ + u * P:(2 + h) * SEQ + (u + 1) * P], gs_[:, h, u // GSUB, u % GSUB, :], ident[:])
                    mm.then_inc(S("ss_gp"), 1)
                e.wait_ge(S("ss_uc"), i + 1)
                for h in range(2):
                    e.wait_ge(S("ss_gt"), i * 2 + (h + 1))
                for h in range(2):
                    for u in range(2 * GSUB):
                        mm = e.matmul(PSr[:, (2 + h) * SEQ + u * P:(2 + h) * SEQ + (u + 1) * P], gT[:, h, u // GSUB, u % GSUB, :],
                                      uT[:, u % GSUB, :], start=True, stop=True)
                mm.then_inc(S("ss_v"), 1)
                e.wait_ge(S("km"), i * 128 + 128)
                e.wait_ge(S("ssd"), i * ND + 29)
                for g in range(GSUB):
                    o = PS[:, 3, g * P:(g + 1) * P]
                    e.matmul(o, uT[:, g, :], mm_[:, g, :], start=True, stop=False)
                    for d in range(2):
                        for h in range(2):
                            m0 = 1 if d == 0 else 0
                            mm = e.matmul(o, av[:, h, d, g, :], oo[h][:, d, g, m0:m0 + CH, :].rearrange("p t c -> p (t c)"),
                                          start=False, stop=d == 1 and h == 1)
                mm.then_inc(S("ss_y"), 1)
            ssm_turns(e, turn_)
            e.wait_ge(S("ss_gl"), 1)
            for m in range(3):
                for h in range(2):
                    q = 2 * m + h
                    wait(e, S("ss_ye"), q - 1)
                    for i in range(4):
                        mm = e.transpose(PS[:, q % 2, i * P:(i + 1) * P], y_nat[:, h * 4 + i, m * P:(m + 1) * P], ident[:])
                    mm.then_inc(S("ss_yt"), 1)
            g = G_GLU
            e.wait_ge(S("w_split"), g + 1)
            e.wait_ge(S("ss_yl"), 3)
            wh, wl = w_view(g % NBUF, "glu", "hi"), w_view(g % NBUF, "glu", "lo")
            for m in range(3):
                for k in range(3):
                    mm = three(e, [PS[:, 2 * (m + 1) + h, :] for h in range(2)],
                               (wh[:, k, m * P:(m + 1) * P], wl[:, k, m * P:(m + 1) * P]),
                               [(y_hi[:, k, h * 512:(h + 1) * 512], y_lo[:, k, h * 512:(h + 1) * 512]) for h in range(2)],
                               k == 0, k == 2)
                mm.then_inc(S("w_used") if m == 2 else S("gl_mm"), 1)

        def ssm_dve(e):
            for par in range(2):
                e.wait_ge(S(f"z_st{par}"), z_stores(0, par))
            e.memset(av[:], 0.0).then_inc(S("ssd"), 1)
            e.wait_ge(S("ss_ld"), 16)
            e.tensor_tensor(y_nat[:], u_nat[:], drow[:].unsqueeze(1).to_broadcast([P, CH, SSM_W]), ALU.mult)\
             .then_inc(S("ss_du"), 1)
            e.wait_ge(S("ss_du"), 1)

            def turn_(i, j, turn):
                g0 = i * GSUB
                ch = Chain(e, S("ssd"), i * ND + 1)
                wait(e, S("ss_y"), i)
                wait(e, S("ss_k"), i)
                for d in range(2):
                    qr, qi = (PR, PI) if d == 0 else (PRD, PID)
                    r, m = (st4(q, 9, d, g0).rearrange("p t g -> p g t").unsqueeze(3).to_broadcast([P, GSUB, 9, GC])
                            for q in (qr, qi))
                    c1, c2 = (cc[k][:].rearrange("p (g c) -> p g c", c=GC)[:, ds(g0, GSUB), :].unsqueeze(2)
                              .to_broadcast([P, GSUB, 9, GC]) for k in range(2))
                    for k, (x0, x1, op) in enumerate((((r, c1), (m, c2), ALU.add), ((r, c2), (m, c1), ALU.subtract))):
                        for y, (a, b) in enumerate((x0, x1)):
                            ch.then(e.tensor_tensor(ot[y][:], a, b, ALU.mult))
                        ch.then(e.tensor_tensor(oo[k][:, d], ot[0][:], ot[1][:], op))
                e.wait_ge(S("ss_v"), i + 1)
                e.wait_ge(S("ssp"), i * NPL + NPL)
                v, w = (PSr[:, (2 + h) * SEQ:(3 + h) * SEQ].rearrange("p (u n) -> p u n", n=P) for h in range(2))
                ch.then(e.tensor_tensor(t1[:], v, cosn[:], ALU.mult))
                ch.then(e.tensor_tensor(t2[:], w, sinn[:], ALU.mult))
                f, b = slice(0, GSUB), slice(GSUB, 2 * GSUB)
                ch.then(e.tensor_tensor(t1[:, f], t1[:, f], t2[:, f], ALU.add))
                ch.then(e.tensor_tensor(t1[:, b], t1[:, b], t2[:, b], ALU.subtract))
                for u in range(2 * GSUB):
                    rho = stn[:, RHO, ds(g0 + (u // GSUB * G + u % GSUB), 1)].to_broadcast([P, P])
                    o, x = (t2[:, u, :], t1[:, u, :]) if u < GSUB else (t2[:, u, ::-1], t1[:, u, ::-1])
                    ch.then(e.tensor_tensor_scan(o, rho, x, 0.0, ALU.mult, ALU.add))
                n1 = P - 1
                ch.then(e.tensor_tensor(av[:, 0, 0, :, 1:], cosn[:, f, 0:n1], t2[:, f, 0:n1], ALU.mult))
                ch.then(e.tensor_tensor(av[:, 1, 0, :, 1:], sinn[:, f, 0:n1], t2[:, f, 0:n1], ALU.mult))
                ch.then(e.tensor_tensor(av[:, 0, 1, :, 0:n1], cosn[:, b, 1:], t2[:, b, 1:], ALU.mult))
                ch.then(e.scalar_tensor_tensor(av[:, 1, 1, :, 0:n1], sinn[:, b, 1:], -1.0, t2[:, b, 1:], ALU.mult, ALU.mult))
                e.wait_ge(S("ss_y"), i + 1)
                yn = y_nat[:].rearrange("p t (g c) -> p g t c", c=GC)[:, ds(g0, GSUB)]
                ch.then(e.tensor_tensor(yn, yn, PS[:, 3, :].rearrange("p (g t c) -> p g t c", g=GSUB, c=GC), ALU.add))
                assert ch.n == ND, ch.n
            ssm_turns(e, turn_)
            e.memset(junk[:, 1:2], 0.0).then_inc(S("ssd"), 1)
            for m in range(3):
                e.wait_ge(S("ss_yh"), m + 1)
                e.tensor_tensor(y_lo[:, m, :], yT[:, m, :], y_hi[:, m, :].bitcast(F32), ALU.subtract).then_inc(S("ss_yl"), 1)
            e.wait_ge(S("w_used"), G_GLU + 1)
            for m in range(3):
                e.wait_ge(S("gl_s"), m + 1)
                e.tensor_tensor(yT[:, m, :], yT[:, m, :], sig[:, m, :], ALU.mult).then_inc(S("gl_y"), 1)
                e.wait_ge(S("gl_h"), m + 1)
                e.tensor_tensor(y_lo[:, m, :], yT[:, m, :], y_hi[:, m, :].bitcast(F32), ALU.subtract).then_inc(S("gl_l"), 1)

        class Att:
            def __init__(self, name, z, pairs, per, pair0, slot0, off, width, keys, sink0):
                self.name, self.z, self.pairs, self.per, self.pair0, self.slot0 = name, z, pairs, per, pair0, slot0
                self.off, self.width, self.keys, self.sink0 = off, width, keys, sink0
                self.n0, self.h0 = pair0 * 16, pair0 * 2
                self.units = per * 16
                self.qs = 512 if width <= 512 else 1024
                self.ob = 3 if width <= 512 else 7

        att_bi = Att("bi", 0, 3, 3, 0, 5, 128, 384, lambda b: (max(b - 1, 0), min(b + 2, TT)), 0)
        att_a = Att("a", 1, 4, 2, 3, 0, 128, 256, lambda b: (max(b - 1, 0), b + 1), 6)
        att_b = Att("b", 1, 4, 2, 7, 4, 896, 1024, lambda b: (0, b + 1), None)
        aq = [at(f"aq{i}", [P, SEQ], F32, i * 4 * KB) for i in range(2)]
        ak = [at(f"ak{i}", [P, SEQ], F32, (8 + i * 4) * KB) for i in range(2)]
        avv = [at(f"avv{i}", [P, TT, 2, HD], F32, (16 + i * 4) * KB) for i in range(2)]
        atb = [at(f"atb{i}", [P, 2, 1024], F32, (24 + i * 8) * KB) for i in range(2)]
        pr = [at(f"pr{i}", [P, 1024], F32, (40 + i * 4) * KB) for i in range(2)]
        pt = [at(f"pt{i}", [P, 1024], F32, (48 + i * 4) * KB) for i in range(2)]
        ao = at("ao", [P, 2, 4, P], F32, 56 * KB)
        sk = at("sk", [P, 14], F32, R3 + 7328)
        MX, NM, DEN, ES, DT_, RD = range(6)
        ast = at("ast", [P, 6, 4], F32, R3 + 7392)

        def att_sp(e, s):
            for par in range(2):
                e.wait_ge(S(f"z_st{par}"), z_stores(s.z, par))
            if s.z == 0:
                e.wait_ge(S("gl_l"), 3)
                e.wait_ge(S("gl_h"), 3)
            else:
                for par in range(2):
                    e.wait_ge(S(f"tb_st{par}"), 128)
                e.wait_ge(S("w_used"), G_Z2 + 9)

            def pair(i, j, turn):
                b = j % 2
                wait_alone(e, S("at_o"), i * 16 + 16 * (s.pair0 - 1), S("idc"))
                sem = S(f"at_ld_{s.name}{b}")
                q0 = 640 if s is att_b else 0
                e.dma_start(aq[b][:], qk[ds(i * P + q0, P), :]).then_inc(sem, 16)
                for hh in range(2):
                    if s is att_bi:
                        kr, vc = 384 + (i + hh) // 2 * HD, (i + hh) // 2 * HD
                    elif s is att_a:
                        kr, vc = turn * HD + 512, turn * HD
                    else:
                        kr, vc = i * P + (1152 + hh * HD), i * P + (P + hh * HD)
                    e.dma_start(ak[b][hh * HD:(hh + 1) * HD, :], qk[ds(kr, HD), :]).then_inc(sem, 16)
                    e.dma_start(avv[b][:, :, hh, :], vs.rearrange("(t p) n -> p t n", p=P)[:, :, ds(vc, HD)]).then_inc(sem, 16)
                if s is att_bi:
                    tab = t["bias1"][2 * i:2 * i + 2]
                else:
                    tab = bass.AP(tensor=tabd.tensor, offset=127, ap=[[P * W_B, 16], [W_B - 1, P], [1, s.width]])
                    tab = tab[ds(i * 2 + (8 if s is att_b else 0), 2)]
                e.dma_start(atb[b][:, :, 0:s.width], tab.rearrange("h p w -> p h w")).then_inc(sem, 16)

            repeat(e, s.pairs, s.per, pair)

        def att_geo(s, m):
            b, hh = m % 16 // 2, m % 2
            k0, k1 = s.keys(b)
            return m // 16, b, hh, k0, k1

        def att_ld_wait(e, s, m, t_):
            p = m // 16
            if s is att_bi:
                e.wait_ge(S(f"at_ld_{s.name}{p % 2}"), 96 * (p // 2 + 1))
            else:
                e.wait_ge(S(f"at_ld_{s.name}{p % 2}"), t_ * 96 + 96)

        def att_turns(e, s, body):
            repeat(e, s.pairs // s.per, 1, lambda i, j, turn: body(i))

        def att_pe(e, s):
            if s.z == 0:
                e.wait_ge(S("gl_s"), 3)
            else:
                e.wait_ge(S("z_ev"), len(Z1) + len(Z2))

            def body(t_):
                n = lambda k: t_ * s.units + (s.n0 + k)

                def scores(m):
                    p, b, hh, k0, k1 = att_geo(s, m)
                    if m % 16 == 0:
                        att_ld_wait(e, s, m, t_)
                    wait(e, S("at_s"), n(m - 1))
                    r = slice(hh * HD, (hh + 1) * HD)
                    for c in range(k0 * P, k1 * P, 512):
                        c1 = min(c + 512, k1 * P)
                        o = m % 2 * s.qs + c - k0 * P
                        mm = e.matmul(PSr[:, o:o + c1 - c], aq[p % 2][r, b * P:(b + 1) * P], ak[p % 2][r, c:c1],
                                      start=True, stop=True)
                    mm.then_inc(S("at_qk"), 1)

                def turn_p(m):
                    _, _, _, k0, k1 = att_geo(s, m)
                    e.wait_ge(S("at_exp"), n(m + 1))
                    wait(e, S("at_pt"), n(m))
                    for k in range(k1 - k0):
                        mm = e.transpose(PSr[:, 2048 + k * P:2048 + (k + 1) * P], pr[m % 2][:, k * P:(k + 1) * P], ident[:])
                    mm.then_inc(S("at_tr"), 1)

                def values(m):
                    p, b, hh, k0, k1 = att_geo(s, m)
                    e.wait_ge(S("at_pt"), n(m + 1))
                    wait(e, S("at_o"), n(m - 1))
                    o = PS[:, 6 + m % 2, 0:HD]
                    if m % 8 == 1:
                        wait(e, S("at_yl"), t_ * (s.units // 8) + (s.h0 + m // 8))
                    for k in range(k1 - k0):
                        mm = e.matmul(o, pt[m % 2][:, k * P:(k + 1) * P], avv[p % 2][:, k0 + k, hh, :],
                                      start=k == 0, stop=k == k1 - k0 - 1)
                    mm.then_inc(S("at_pv"), 1)

                def turn_o(h):
                    e.wait_ge(S("at_o"), n(8 * h + 8))
                    wait(e, S("at_yl"), t_ * (s.units // 8) + (s.h0 + h))
                    for k in range(4):
                        mm = e.transpose(PS[:, s.ob, k * P:(k + 1) * P], ao[:, h % 2, k, :], ident[:])
                    mm.then_inc(S("at_ot"), 1)

                scores(0)
                scores(1)
                for m in range(s.units):
                    turn_p(m)
                    if m:
                        values(m - 1)
                    if m + 2 < s.units:
                        scores(m + 2)
                    if m >= 9 and m % 8 == 1:
                        turn_o(m // 8 - 1)
                values(s.units - 1)
                turn_o(s.units // 8 - 1)

            att_turns(e, s, body)

        def att_act(e, s):
            if s.z:
                e.wait_ge(S("w_used"), G_Z2 + 9)

            def body(t_):
                n = lambda k: t_ * s.units + (s.n0 + k)

                def exps(m):
                    _, _, _, k0, k1 = att_geo(s, m)
                    x, r = pr[m % 2][:, 0:(k1 - k0) * P], m % 4
                    wait_alone(e, S("at_nm"), n(m + 1), S("idc"))
                    if s.sink0 is not None:
                        i = t_ * (2 * s.per) + (s.sink0 + m // 16 * 2 + m % 2)
                        e.activation(ast[:, ES, r:r + 1], sk[:, ds(i, 1)], ACT.Exp, bias=ast[:, NM, r:r + 1])\
                         .then_inc(S("at_es"), 1)
                    e.activation(x, x, ACT.Exp, bias=ast[:, NM, r:r + 1], accum_out=ast[:, DEN, r:r + 1])\
                     .then_inc(S("at_exp"), 1)

                def move_p(m):
                    _, _, _, k0, k1 = att_geo(s, m)
                    w = (k1 - k0) * P
                    e.wait_ge(S("at_tr"), n(m + 1))
                    wait(e, S("at_pv"), n(m - 1))
                    e.activation(pt[m % 2][:, 0:w], PSr[:, 2048:2048 + w], ACT.Copy).then_inc(S("at_pt"), 1)

                def y_high(h):
                    wait_alone(e, S("at_ot"), t_ * (s.units // 8) + (s.h0 + h + 1), S("idc"))
                    e.activation(y_hi[:, ds(t_ * s.per + (s.slot0 + h // 2), 1), h % 2 * 512:(h % 2 + 1) * 512]
                                 .rearrange("p o n -> p (o n)"), PS[:, s.ob, :], ACT.Copy).then_inc(S("at_yh"), 1)

                exps(0)
                for m in range(s.units):
                    if m + 1 < s.units:
                        exps(m + 1)
                    move_p(m)
                    if m >= 9 and m % 8 == 1:
                        y_high(m // 8 - 1)
                y_high(s.units // 8 - 1)

            att_turns(e, s, body)

        def att_dve(e, s):
            if s.sink0 is not None:
                e.wait_ge(S("sk_ld"), 32)

            def body(t_):
                n = lambda k: t_ * s.units + (s.n0 + k)

                def score(m):
                    p, b, hh, k0, k1 = att_geo(s, m)
                    w, r, j0 = (k1 - k0) * P, m % 4, (k0 - b) * P + s.off
                    if m % 16 == 0:
                        att_ld_wait(e, s, m, t_)
                    wait(e, S("at_tr"), n(m - 1))
                    wait_alone(e, S("at_qk"), n(m + 1), S("idc"))
                    e.tensor_tensor_reduce(out=pr[m % 2][:, 0:w], in0=PSr[:, m % 2 * s.qs:m % 2 * s.qs + w],
                                           in1=atb[p % 2][:, hh, j0:j0 + w], scale=1.0, scalar=3 * NEG, op0=ALU.add,
                                           op1=ALU.max, accum_out=ast[:, MX, r:r + 1]).then_inc(S("at_s"), 1)
                    e.wait_ge(S("at_s"), n(m + 1))
                    i = t_ * (2 * s.per) + ((s.sink0 or 0) + m // 16 * 2 + m % 2)
                    if s.sink0 is None:
                        e.tensor_scalar(ast[:, NM, r:r + 1], ast[:, MX, r:r + 1], -1.0, None, ALU.mult).then_inc(S("at_nm"), 1)
                    else:
                        e.tensor_scalar(ast[:, NM, r:r + 1], ast[:, MX, r:r + 1], sk[:, ds(i, 1)], -1.0, ALU.max, ALU.mult)\
                         .then_inc(S("at_nm"), 1)

                def finish(m):
                    r, q = m % 4, DEN
                    e.wait_ge(S("at_exp"), n(m + 1))
                    if s.sink0 is not None:
                        e.tensor_tensor(ast[:, DT_, r:r + 1], ast[:, DEN, r:r + 1], ast[:, ES, r:r + 1], ALU.add)\
                         .then_inc(S("at_dn"), 1)
                        e.wait_ge(S("at_dn"), n(m + 1))
                        q = DT_
                    e.reciprocal(ast[:, RD, r:r + 1], ast[:, q, r:r + 1]).then_inc(S("at_rd"), 1)
                    e.wait_ge(S("at_rd"), n(m + 1))
                    e.wait_ge(S("at_pv"), n(m + 1))
                    if m % 8 == 0:
                        wait(e, S("at_ot"), t_ * (s.units // 8) + (s.h0 + m // 8 - 1))
                    e.tensor_scalar(ao[:, m // 8 % 2, m % 8 // 2, m % 2 * HD:(m % 2 + 1) * HD],
                                    PS[:, 6 + m % 2, 0:HD], ast[:, RD, r:r + 1], None, ALU.mult)\
                     .then_inc(S("at_o"), 1)

                def y_low(h):
                    e.wait_ge(S("at_yh"), t_ * (s.units // 8) + (s.h0 + h + 1))
                    a = (slice(None), ds(t_ * s.per + (s.slot0 + h // 2), 1), slice(h % 2 * 512, (h % 2 + 1) * 512))
                    e.tensor_tensor(y_lo[a].rearrange("p o n -> p (o n)"), PS[:, s.ob, :],
                                    y_hi[a].rearrange("p o n -> p (o n)").bitcast(F32), ALU.subtract).then_inc(S("at_yl"), 1)

                score(0)
                for m in range(s.units):
                    if m + 1 < s.units:
                        score(m + 1)
                    if m:
                        finish(m - 1)
                    if m >= 9 and m % 8 == 1:
                        y_low(m // 8 - 1)
                finish(s.units - 1)
                y_low(s.units // 8 - 1)

            att_turns(e, s, body)

        gs = at("gs", [P, 4, D], F32, 0)
        p_hi = at("p_hi", [P, 2, SEQ], F32R, 16 * KB)
        p_lo = at("p_lo", [P, 2, SEQ], F32R, 24 * KB)
        p_nat = at("p_nat", [P, TT, 256], F32, 32 * KB)

        def ple_sp(e):
            e.wait_ge(S("w_used"), G_PLE[0])
            e.dma_start(p_nat[:], t["p_2"][0, 0].rearrange("(t p) n -> p t n", p=P)).then_inc(S("pl_ld"), 16)

        def ple_pe(e):
            e.wait_ge(S("pl_ld"), 16)
            for k in range(2):
                for T in range(TT):
                    mm = e.transpose(PSr[:, 1024 * (k + 1) + T * P:1024 * (k + 1) + (T + 1) * P], p_nat[:, T, k * P:(k + 1) * P], ident[:])
            mm.then_inc(S("pl_t"), 1)
            e.wait_ge(S("ht_lo"), 16 * 6)
            e.wait_ge(S("pl_lo"), 1)
            for grp in range(2):
                g0 = G_PLE[grp]
                for m in range(4):
                    rows_chunk_pe(e, g0 + m, (g0 + m) % NBUF, from_tiles(h_hi, h_lo, 2 * m, grp),
                                  ("n_y", 8) if grp else None, m == 0, m == 3, -1)
                rows_chunk_pe(e, g0 + 4, (g0 + 4) % NBUF, from_tiles(p_hi, p_lo, 0, grp), ("gs", grp * 4), True, True, 5)

        def ple_act(e):
            e.wait_ge(S("pl_t"), 1)
            e.activation(p_hi[:].rearrange("p k n -> p (k n)"), PSr[:, 1024:3072], ACT.Copy).then_inc(S("pl_hi"), 1)
            post_load_act(e, 5)
            for grp in range(2):
                for k in range(4):
                    if k < 3:
                        e.wait_ge(S("gate_rdy"), grp * 3 + k + 1)
                    else:
                        e.wait_ge(S("w_used"), G_PLE[grp] + 4)
                    if grp:
                        e.wait_ge(S("n_y"), 8 + k + 1)
                    e.activation(gs[:, k, :], ys(k), ACT.Sigmoid).then_inc(S("gs"), 1)
                for k in range(4):
                    post_sq_act(e, 5, grp * 4 + k)
                    post_store_act(e, 5, grp * 4 + k)

        def ple_dve(e):
            e.wait_ge(S("pl_hi"), 1)
            e.tensor_tensor(p_lo[:].rearrange("p k n -> p (k n)"), PSr[:, 1024:3072],
                            p_hi[:].rearrange("p k n -> p (k n)").bitcast(F32), ALU.subtract).then_inc(S("pl_lo"), 1)
            for T in range(TT):
                post_dve(e, 5, T)

        n_vr = N_VR
        with nc.Block() as block:

            @block.sync
            def _(e):
                assert prep_sp(e) == n_vr
                stream_load(e, NBUF, G_GLU + NBUF)
                ssm_sp(e)
                att_sp(e, att_bi)
                if last > 3:
                    stream_load(e, G_GLU + NBUF, G_OUT2[0] + NBUF)
                    att_sp(e, att_a)
                    att_sp(e, att_b)
                    if last > 5:
                        stream_load(e, G_OUT2[0] + NBUF, G_PLE[0] + NBUF)
                        ple_sp(e)
                        stream_load(e, G_PLE[0] + NBUF, g_end)
                    else:
                        stream_load(e, G_OUT2[0] + NBUF, g_end)
                else:
                    stream_load(e, G_GLU + NBUF, g_end)
                e.wait_ge(S("x_st"), 16 * TT * last)

            @block.gpsimd
            def _(e):
                prep_pool(e)
                stream_split(e, 0, G_GLU)
                ssm_pool(e)
                stream_split(e, G_GLU, g_end)

            @block.tensor
            def _(e):
                prep_pe(e)
                norm_pe(e, 0)
                z_pe(e, 0)
                fft_pe(e)
                ssm_pe(e)
                att_pe(e, att_bi)
                out_pe(e, 0)
                for f, p in ((0, 1), (1, 2)):
                    if last > p:
                        norm_pe(e, NORM_OF[f])
                        up_pe(e, f)
                        down_pe(e, p)
                if last > 3:
                    norm_pe(e, 3)
                    z_pe(e, 1)
                    att_pe(e, att_a)
                    att_pe(e, att_b)
                    out_pe(e, 3)
                if last > 4:
                    norm_pe(e, 4)
                    up_pe(e, 2)
                    down_pe(e, 4)
                if last > 5:
                    norm_pe(e, 5)
                    ple_pe(e)

            @block.scalar
            def _(e):
                e.dma_start(sk[:, 0:6], t["sink"][0].partition_broadcast(P)).then_inc(S("sk_ld"), 16)
                e.dma_start(sk[:, 6:14], t["sinks_2"][0].partition_broadcast(P)).then_inc(S("sk_ld"), 16)
                prep_act(e)
                prep_act_end(e)
                for T in range(TT):
                    norm_sq_act(e, 0, T)
                for T in range(TT):
                    norm_scale_act(e, 0, T)
                norm_out_act(e, 0)
                fft_loads(e)
                z_act(e, 0)
                fft_act(e)
                ssm_act(e)
                e.wait_ge(S("sk_ld"), 32)
                att_act(e, att_bi)
                out_act(e, 0)
                for f, p in ((0, 1), (1, 2)):
                    if last > p:
                        up_act(e, f)
                        down_act(e, p)
                if last > 3:
                    z_act(e, 1)
                    att_act(e, att_a)
                    att_act(e, att_b)
                    out_act(e, 3)
                if last > 4:
                    up_act(e, 2)
                    down_act(e, 4)
                if last > 5:
                    ple_act(e)

            @block.vector
            def _(e):
                prep_dve(e)
                for T in range(TT):
                    norm_r_dve(e, 0, T)
                norm_out_dve(e, 0)
                z_dve(e, 0)
                fft_dve(e)
                ssm_dve(e)
                att_dve(e, att_bi)
                out_dve(e, 0)
                for f, p in ((0, 1), (1, 2)):
                    if last > p:
                        up_dve(e, f)
                        down_dve(e, p)
                if last > 3:
                    z_dve(e, 1)
                    att_dve(e, att_a)
                    att_dve(e, att_b)
                    out_dve(e, 3)
                if last > 4:
                    up_dve(e, 2)
                    down_dve(e, 4)
                if last > 5:
                    ple_dve(e)


def constants():
    import math
    import numpy as np
    f = np.float32
    n = np.arange(SEQ)
    ang = 2 * np.pi * (np.outer(n, n) % SEQ) / SEQ
    dft = np.stack([np.cos(ang).reshape(TT, P, SEQ), -np.sin(ang).reshape(TT, P, SEQ)], 1).reshape(2 * SEQ, SEQ)
    h = np.arange(HD)
    angh = 2 * np.pi * (np.outer(h, h) % HD) / HD
    head = np.zeros((P, 2, P))
    for a in range(2):
        s = slice(a * HD, (a + 1) * HD)
        head[s, 0, s], head[s, 1, s] = np.cos(angh), np.sin(angh)
    dist = np.abs(np.arange(P)[:, None] + P - np.arange(3 * P)[None, :])
    slopes = np.exp2(f(-8.0) * np.arange(1, 7, dtype=f) / f(6))
    bias1 = np.where(dist <= P, -slopes[:, None, None] * dist.astype(f), f(NEG))

    def one_hot(first, width, count):
        d = first - np.arange(width)
        nf = np.maximum(d, 1).astype(f)
        large = 16 + (np.log(nf / f(16)) / f(math.log(2048 / 16)) * f(16)).astype(np.int32)
        bucket = np.where(d < 16, np.maximum(d, 0), np.minimum(large, BUCKETS - 1))
        oh = np.zeros((BUCKETS + 1, width), f)
        oh[bucket, np.arange(width)] = 1
        c = count(d) * (d >= 0)
        oh[BUCKETS] = np.where(c > 0, np.log(np.maximum(c, 1)), NEG)
        return oh

    oh_a = one_hot(255, W_A, lambda d: d <= 127)
    oh_b = one_hot(1023, W_B, lambda d: (d <= 128) * 1 + (d % 4 == 0) * (d <= 512) + (d % 16 == 0) * (d <= 2048))
    return {"dft": dft.astype(f), "dft_head": head.astype(f), "bias1": bias1.astype(f), "oh_a": oh_a, "oh_b": oh_b}


def kernel(**inputs):
    import numpy as np
    import concourse.bacc as _bacc
    from concourse.bass_utils import run_bass_kernel_spmd

    arrays = {k: np.ascontiguousarray(v) for k, v in inputs.items()}
    arrays.update(constants())
    nc = _bacc.Bacc("TRN2", target_bir_lowering=False, num_devices=1)
    t = {k: nc.dram_tensor(k, v.shape, F32, kind="ExternalInput").ap() for k, v in arrays.items()}
    out = nc.dram_tensor("out", (1, SEQ, D), F32, kind="ExternalOutput").ap()
    build(nc, t, out)
    nc.compile()
    r = run_bass_kernel_spmd(nc, [arrays], core_ids=[0])
    return r.results[0]["out"]
```
